# Optimizing a Trainium2 kernel written in Bass

```python
import jax, jax.numpy as jnp
from jax import lax
import numpy as np
import math

D_MODEL = 1024
BATCH = 1
SEQ = 256
DEPTH = 2

N_A_LAYERS = DEPTH // 2
N_B_LAYERS = DEPTH - N_A_LAYERS
N_SUBLAYERS = 3
GLA_HEADS = 4
GLA_DK = D_MODEL // 2 // GLA_HEADS
GLA_DV = D_MODEL // GLA_HEADS
GLA_GATE_RANK = 16
GLA_TAU = 16.0
GLA_CHUNK = 64
MLA_HEADS = 8
QK_NOPE = 128
QK_ROPE = 64
V_HEAD = 128
KV_LORA = 256
Q_LORA = 384
ROPE_THETA = 10000.0
Q_BLOCK = 128
D_FF = 2816
EPS = 1e-6
MAX_POS_OFFSET = 1024


def rmsnorm(x, g):
    xf = x.astype(jnp.float32)
    y = xf * lax.rsqrt(jnp.mean(xf * xf, axis=-1, keepdims=True) + EPS)
    return (y * g.astype(jnp.float32)).astype(x.dtype)

def swiglu(h, w_gu, w_down):
    gate, up = jnp.split(h @ w_gu, 2, axis=-1)
    return (jax.nn.silu(gate) * up) @ w_down

def sublayer(x, shift, scale, gate, g_pre, g_post, fn, res_weight):
    h = rmsnorm(x, g_pre) * (1 + scale[:, None, :]) + shift[:, None, :]
    return x + res_weight * gate[:, None, :] * rmsnorm(fn(h), g_post)

def rope_tables(positions):
    inv_freq = ROPE_THETA ** (-jnp.arange(0, QK_ROPE, 2, dtype=jnp.float32) / QK_ROPE)
    ang = positions.astype(jnp.float32)[..., None] * inv_freq
    return jnp.cos(ang), jnp.sin(ang)

def apply_rope(x, cos, sin):
    cos = cos.astype(x.dtype)
    sin = sin.astype(x.dtype)
    x1, x2 = jnp.split(x, 2, axis=-1)
    return jnp.concatenate([x1 * cos - x2 * sin, x1 * sin + x2 * cos], axis=-1)

def gla_chunked(q, k, v, log_a):
    B, S, H, DK = q.shape
    C = GLA_CHUNK
    N = S // C
    f32 = jnp.float32

    def chunks(t):
        return t.astype(f32).reshape(B, N, C, H, t.shape[-1]).transpose(0, 3, 1, 2, 4)

    q, k, v, log_a = chunks(q) * DK ** -0.5, chunks(k), chunks(v), chunks(log_a)
    b = jnp.cumsum(log_a, axis=3)
    b_last = b[:, :, :, -1:, :]
    q_dec = q * jnp.exp(b)
    k_dec = k * jnp.exp(-b)
    causal = jnp.tril(jnp.ones((C, C), dtype=bool))
    att = jnp.where(causal, jnp.einsum('bhnid,bhnjd->bhnij', q_dec, k_dec), 0.0)
    o_intra = jnp.einsum('bhnij,bhnjv->bhniv', att, v)
    upd = jnp.einsum('bhncd,bhncv->bhndv', k * jnp.exp(b_last - b), v)
    decay = jnp.exp(b_last[:, :, :, 0, :])

    def step(state, inp):
        dec, u = inp
        return dec[..., None] * state + u, state

    s0 = jnp.zeros((B, H, DK, v.shape[-1]), f32)
    _, states = lax.scan(step, s0, (jnp.moveaxis(decay, 2, 0), jnp.moveaxis(upd, 2, 0)))
    states = jnp.moveaxis(states, 0, 2)
    o = o_intra + jnp.einsum('bhncd,bhndv->bhncv', q_dec, states)
    return o.transpose(0, 2, 3, 1, 4).reshape(B, S, H, v.shape[-1])

def gla_mixer(h, w_in, w_gate_up, b_gate, g_out, w_out):
    B, S, _ = h.shape
    kd = GLA_HEADS * GLA_DK
    vd = GLA_HEADS * GLA_DV
    q, k, v, g_low, r = jnp.split(h @ w_in, [kd, 2 * kd, 2 * kd + vd, 2 * kd + vd + GLA_GATE_RANK], axis=-1)
    log_a = jax.nn.log_sigmoid((g_low @ w_gate_up + b_gate).astype(jnp.float32)) / GLA_TAU
    o = gla_chunked(q.reshape(B, S, GLA_HEADS, GLA_DK), k.reshape(B, S, GLA_HEADS, GLA_DK),
                    v.reshape(B, S, GLA_HEADS, GLA_DV), log_a.reshape(B, S, GLA_HEADS, GLA_DK))
    o = rmsnorm(o, g_out).astype(h.dtype).reshape(B, S, vd)
    return (o * jax.nn.silu(r)) @ w_out

def mla_shared_kv(h, w_kv_a, g_kv, w_kv_b, cos, sin):
    B, S, _ = h.shape
    c_kv, k_pe = jnp.split(h @ w_kv_a, [KV_LORA], axis=-1)
    c_kv = rmsnorm(c_kv, g_kv)
    k_rope = apply_rope(k_pe, cos, sin)
    kv = (c_kv @ w_kv_b).reshape(B, S, MLA_HEADS, QK_NOPE + V_HEAD)
    k_nope, v = jnp.split(kv, [QK_NOPE], axis=-1)
    return k_nope, k_rope, v

def mla_mixer(h, k_nope, k_rope, v, w_dq, g_q, w_uq, w_out, cos, sin):
    B, S, _ = h.shape
    c_q = rmsnorm(h @ w_dq, g_q)
    q = (c_q @ w_uq).reshape(B, S, MLA_HEADS, QK_NOPE + QK_ROPE)
    q_nope, q_rope = jnp.split(q, [QK_NOPE], axis=-1)
    q_rope = apply_rope(q_rope, cos[:, :, None, :], sin[:, :, None, :])
    scale = (QK_NOPE + QK_ROPE) ** -0.5
    nb = S // Q_BLOCK
    qn_blocks = q_nope.reshape(B, nb, Q_BLOCK, MLA_HEADS, QK_NOPE).transpose(1, 0, 2, 3, 4)
    qr_blocks = q_rope.reshape(B, nb, Q_BLOCK, MLA_HEADS, QK_ROPE).transpose(1, 0, 2, 3, 4)
    key_pos = jnp.arange(S)
    neg = jnp.finfo(jnp.float32).min

    def attend(args):
        qn, qr, blk = args
        s = (jnp.einsum('bqhd,bkhd->bhqk', qn, k_nope) +
             jnp.einsum('bqhr,bkr->bhqk', qr, k_rope)).astype(jnp.float32) * scale
        q_pos = blk * Q_BLOCK + jnp.arange(Q_BLOCK)
        s = jnp.where(key_pos[None, :] <= q_pos[:, None], s, neg)
        p = jax.nn.softmax(s, axis=-1).astype(v.dtype)
        return jnp.einsum('bhqk,bkhv->bqhv', p, v)

    o = lax.map(attend, (qn_blocks, qr_blocks, jnp.arange(nb)))
    o = o.transpose(1, 0, 2, 3, 4).reshape(B, S, MLA_HEADS * V_HEAD)
    return o @ w_out

def first_inputs(seed: int = 0) -> dict:
    key = jax.random.key(seed)
    ks = jax.random.split(key, 24)
    D = D_MODEL
    f32 = jnp.float32

    def w(k, shape, fan_in):
        return jax.random.normal(k, shape, f32) * fan_in ** -0.5

    def gain(k, shape):
        return 1.0 + 0.1 * jax.random.normal(k, shape, f32)

    def bias(k, shape):
        return 0.01 * jax.random.normal(k, shape, f32)

    gla_in_cols = 2 * GLA_HEADS * GLA_DK + 2 * GLA_HEADS * GLA_DV + GLA_GATE_RANK
    offsets = jax.random.randint(ks[2], (BATCH, 1), 0, MAX_POS_OFFSET, dtype=jnp.int32)
    return {
        'x': jax.random.normal(ks[0], (BATCH, SEQ, D), f32),
        'c': jax.random.normal(ks[1], (BATCH, D), f32),
        'positions': offsets + jnp.arange(SEQ, dtype=jnp.int32)[None, :],
        'cond_w': w(ks[3], (DEPTH, D, 3 * N_SUBLAYERS * D), D),
        'cond_b': bias(ks[4], (DEPTH, 3 * N_SUBLAYERS * D)),
        'norm_g': gain(ks[5], (DEPTH, N_SUBLAYERS, 2, D)),
        'ffn_w_gu': w(ks[6], (DEPTH, 2, D, 2 * D_FF), D),
        'ffn_w_down': w(ks[7], (DEPTH, 2, D_FF, D), D_FF),
        'gla_w_in': w(ks[8], (N_A_LAYERS, D, gla_in_cols), D),
        'gla_w_gate_up': w(ks[9], (N_A_LAYERS, GLA_GATE_RANK, GLA_HEADS * GLA_DK), GLA_GATE_RANK),
        'gla_b_gate': 0.1 * jax.random.normal(ks[10], (N_A_LAYERS, GLA_HEADS * GLA_DK), f32),
        'gla_g_out': gain(ks[11], (N_A_LAYERS, GLA_DV)),
        'gla_w_out': w(ks[12], (N_A_LAYERS, GLA_HEADS * GLA_DV, D), GLA_HEADS * GLA_DV),
        'kv_g_in': gain(ks[13], (D,)),
        'kv_cond_w': w(ks[14], (D, 2 * D), D),
        'kv_cond_b': bias(ks[15], (2 * D,)),
        'mla_w_kv_a': w(ks[16], (D, KV_LORA + QK_ROPE), D),
        'mla_g_kv': gain(ks[17], (KV_LORA,)),
        'mla_w_kv_b': w(ks[18], (KV_LORA, MLA_HEADS * (QK_NOPE + V_HEAD)), KV_LORA),
        'mla_w_dq': w(ks[19], (N_B_LAYERS, D, Q_LORA), D),
        'mla_g_q': gain(ks[20], (N_B_LAYERS, Q_LORA)),
        'mla_w_uq': w(ks[21], (N_B_LAYERS, Q_LORA, MLA_HEADS * (QK_NOPE + QK_ROPE)), Q_LORA),
        'mla_w_out': w(ks[22], (N_B_LAYERS, MLA_HEADS * V_HEAD, D), MLA_HEADS * V_HEAD),
    }

def first_block(x, c, positions, cond_w, cond_b, norm_g, ffn_w_gu, ffn_w_down,
              gla_w_in, gla_w_gate_up, gla_b_gate, gla_g_out, gla_w_out,
              kv_g_in, kv_cond_w, kv_cond_b, mla_w_kv_a, mla_g_kv, mla_w_kv_b,
              mla_w_dq, mla_g_q, mla_w_uq, mla_w_out):
    cos, sin = rope_tables(positions)
    c_act = jax.nn.silu(c)
    k_nope = k_rope = v_shared = None
    for layer in range(DEPTH):
        mods = jnp.split(c_act @ cond_w[layer] + cond_b[layer], 3 * N_SUBLAYERS, axis=-1)
        g = norm_g[layer]
        x = sublayer(x, mods[0], mods[1], mods[2], g[0, 0], g[0, 1],
                     lambda h: swiglu(h, ffn_w_gu[layer, 0], ffn_w_down[layer, 0]), 0.5)
        if layer < N_A_LAYERS:
            i = layer
            x = sublayer(x, mods[3], mods[4], mods[5], g[1, 0], g[1, 1],
                         lambda h: gla_mixer(h, gla_w_in[i], gla_w_gate_up[i], gla_b_gate[i],
                                             gla_g_out[i], gla_w_out[i]), 1.0)
        else:
            i = layer - N_A_LAYERS
            x = sublayer(x, mods[3], mods[4], mods[5], g[1, 0], g[1, 1],
                         lambda h: mla_mixer(h, k_nope, k_rope, v_shared, mla_w_dq[i], mla_g_q[i],
                                             mla_w_uq[i], mla_w_out[i], cos, sin), 1.0)
        x = sublayer(x, mods[6], mods[7], mods[8], g[2, 0], g[2, 1],
                     lambda h: swiglu(h, ffn_w_gu[layer, 1], ffn_w_down[layer, 1]), 0.5)
        if layer == N_A_LAYERS - 1:
            kv_shift, kv_scale = jnp.split(c_act @ kv_cond_w + kv_cond_b, 2, axis=-1)
            h_kv = rmsnorm(x, kv_g_in) * (1 + kv_scale[:, None, :]) + kv_shift[:, None, :]
            k_nope, k_rope, v_shared = mla_shared_kv(h_kv, mla_w_kv_a, mla_g_kv, mla_w_kv_b, cos, sin)
    return x


N_MIXERS = 2
N_CONV_LAYERS = (DEPTH + N_MIXERS - 1) // N_MIXERS
N_ATTN_LAYERS = DEPTH // N_MIXERS
CONV_WIDTH = 3
ATT_HEADS = 8
ATT_HEAD_DIM = D_MODEL // (2 * ATT_HEADS)
PEER_HEADS = 8
PEER_KEYS = 128
PEER_N_EXPERTS = PEER_KEYS * PEER_KEYS
PEER_TOPK = 16
PEER_QK_DIM = 256
PEER_HALF = PEER_QK_DIM // 2
PEER_CHUNK = 128
DEEPNORM_ALPHA = (2.0 * DEPTH) ** 0.25
DEEPNORM_BETA = (8.0 * DEPTH) ** -0.25
LN_EPS = 1e-5


def layer_norm(x, g, b):
    xf = x.astype(jnp.float32)
    mu = jnp.mean(xf, axis=-1, keepdims=True)
    var = jnp.mean(jnp.square(xf - mu), axis=-1, keepdims=True)
    return ((xf - mu) * lax.rsqrt(var + LN_EPS)).astype(x.dtype) * g + b

def rms_norm(x, g):
    xf = x.astype(jnp.float32)
    return (xf * lax.rsqrt(jnp.mean(xf * xf, axis=-1, keepdims=True) + LN_EPS)).astype(x.dtype) * g

def ada_mod(c, w, b):
    m = jax.nn.silu(c) @ w + b
    shift, scale, gate = jnp.split(m, 3, axis=-1)
    return shift[:, None, :], 1.0 + scale[:, None, :], 1.0 + gate[:, None, :]

def lambda_init_fn(layer_idx):
    return 0.8 - 0.6 * math.exp(-0.3 * layer_idx)

def short_conv_mixer(h, w_in, conv_w, w_out):
    S = h.shape[1]
    gb, gc, xv = jnp.split(h @ w_in, 3, axis=-1)
    z = gc * xv
    zp = jnp.pad(z, ((0, 0), (CONV_WIDTH - 1, 0), (0, 0)))
    zc = conv_w[0] * zp[:, 0:S] + conv_w[1] * zp[:, 1:S + 1] + conv_w[2] * zp[:, 2:S + 2]
    return (gb * zc) @ w_out

def diff_attention(h, w_qkv, lam, subln_g, w_o, lambda_init):
    B, S, _ = h.shape
    H, dh = ATT_HEADS, ATT_HEAD_DIM
    q, k, v = jnp.split(h @ w_qkv, 3, axis=-1)
    q = q.reshape(B, S, H, 2, dh) * (dh ** -0.5)
    k = k.reshape(B, S, H, 2, dh)
    v = v.reshape(B, S, H, 2 * dh)
    lam_f = lam.astype(jnp.float32)
    lam_full = (jnp.exp(jnp.sum(lam_f[0] * lam_f[1])) - jnp.exp(jnp.sum(lam_f[2] * lam_f[3]))
                + lambda_init)
    slopes = 2.0 ** (-(8.0 / H) * jnp.arange(1, H + 1, dtype=jnp.float32))
    kpos = jnp.arange(S)
    nb = S // Q_BLOCK
    qb = q.reshape(B, nb, Q_BLOCK, H, 2, dh).transpose(1, 0, 2, 3, 4, 5)

    def block(args):
        qblk, bi = args
        qpos = bi * Q_BLOCK + jnp.arange(Q_BLOCK)
        s = jnp.einsum('bqhpd,bkhpd->bhpqk', qblk, k).astype(jnp.float32)
        dist = (qpos[:, None] - kpos[None, :]).astype(jnp.float32)
        s = s - slopes[None, :, None, None, None] * dist
        s = jnp.where(dist >= 0, s, -jnp.inf)
        p = jax.nn.softmax(s, axis=-1)
        a = p[:, :, 0] - lam_full * p[:, :, 1]
        return jnp.einsum('bhqk,bkhe->bqhe', a.astype(v.dtype), v)

    o = lax.map(block, (qb, jnp.arange(nb)))
    o = o.transpose(1, 0, 2, 3, 4).reshape(B, S, H, 2 * dh)
    o = rms_norm(o, subln_g) * (1.0 - lambda_init)
    return o.reshape(B, S, H * 2 * dh) @ w_o

def peer_ffn(h, w_q, sub_keys, u, v):
    B, S, D = h.shape
    T = B * S
    hc = h.reshape(T // PEER_CHUNK, PEER_CHUNK, D)

    def chunk(xc):
        q = (xc @ w_q).reshape(PEER_CHUNK, PEER_HEADS, 2, PEER_HALF)
        s = jnp.einsum('thpd,pnd->thpn', q, sub_keys).astype(jnp.float32)
        sv, si = lax.top_k(s, PEER_TOPK)
        cand_s = (sv[:, :, 0, :, None] + sv[:, :, 1, None, :]).reshape(
            PEER_CHUNK, PEER_HEADS, PEER_TOPK * PEER_TOPK)
        cand_i = (si[:, :, 0, :, None] * PEER_KEYS + si[:, :, 1, None, :]).reshape(
            PEER_CHUNK, PEER_HEADS, PEER_TOPK * PEER_TOPK)
        top_s, pos = lax.top_k(cand_s, PEER_TOPK)
        idx = jnp.take_along_axis(cand_i, pos, axis=-1)
        g = jax.nn.softmax(top_s, axis=-1).astype(xc.dtype)
        act = jax.nn.gelu(jnp.einsum('td,thkd->thk', xc, u[idx]), approximate=False)
        return jnp.einsum('thk,thkd->td', g * act, v[idx])

    return lax.map(chunk, hc).reshape(B, S, D)

def second_inputs(seed: int = 0) -> dict:
    key = jax.random.key(seed)
    ks = jax.random.split(key, 20)
    D = D_MODEL
    nrm = jax.random.normal
    f32 = jnp.float32
    x = nrm(ks[0], (BATCH, SEQ, D), f32)
    c = nrm(ks[1], (BATCH, D), f32)
    ada_w = nrm(ks[2], (DEPTH, 2, D, 3 * D), f32) * (0.1 * D ** -0.5)
    ada_b = nrm(ks[3], (DEPTH, 2, 3 * D), f32) * 0.02
    ln_g = 1.0 + 0.02 * nrm(ks[4], (DEPTH, 2, D), f32)
    ln_b = 0.02 * nrm(ks[5], (DEPTH, 2, D), f32)
    val_scale = jnp.concatenate([jnp.ones((2 * D,), f32), jnp.full((D,), DEEPNORM_BETA, f32)])
    conv_w_in = nrm(ks[6], (N_CONV_LAYERS, D, 3 * D), f32) * (D ** -0.5) * val_scale
    conv_w = nrm(ks[7], (N_CONV_LAYERS, CONV_WIDTH, D), f32) * (CONV_WIDTH ** -0.5)
    conv_w_out = nrm(ks[8], (N_CONV_LAYERS, D, D), f32) * (D ** -0.5) * DEEPNORM_BETA
    attn_w_qkv = nrm(ks[9], (N_ATTN_LAYERS, D, 3 * D), f32) * (D ** -0.5) * val_scale
    attn_lambda = 0.1 * nrm(ks[10], (N_ATTN_LAYERS, 4, ATT_HEAD_DIM), f32)
    attn_subln_g = 1.0 + 0.02 * nrm(ks[11], (N_ATTN_LAYERS, 2 * ATT_HEAD_DIM), f32)
    attn_w_o = nrm(ks[12], (N_ATTN_LAYERS, D, D), f32) * (D ** -0.5) * DEEPNORM_BETA
    peer_w_q = nrm(ks[13], (DEPTH, D, PEER_HEADS * PEER_QK_DIM), f32) * (D ** -0.5)
    peer_sub_keys = nrm(ks[14], (DEPTH, 2, PEER_KEYS, PEER_HALF), f32) * (PEER_HALF ** -0.5)
    peer_u = nrm(ks[15], (DEPTH, PEER_N_EXPERTS, D), f32) * (D ** -0.5) * DEEPNORM_BETA
    peer_v = nrm(ks[16], (DEPTH, PEER_N_EXPERTS, D), f32) * (PEER_HEADS ** -0.5) * DEEPNORM_BETA
    return {"x": x, "c": c, "ada_w": ada_w, "ada_b": ada_b, "ln_g": ln_g, "ln_b": ln_b,
            "conv_w_in": conv_w_in, "conv_w": conv_w, "conv_w_out": conv_w_out,
            "attn_w_qkv": attn_w_qkv, "attn_lambda": attn_lambda,
            "attn_subln_g": attn_subln_g, "attn_w_o": attn_w_o,
            "peer_w_q": peer_w_q, "peer_sub_keys": peer_sub_keys,
            "peer_u": peer_u, "peer_v": peer_v}

def second_block(x, c, ada_w, ada_b, ln_g, ln_b, conv_w_in, conv_w, conv_w_out,
              attn_w_qkv, attn_lambda, attn_subln_g, attn_w_o,
              peer_w_q, peer_sub_keys, peer_u, peer_v):
    for i in range(DEPTH):
        j = i // N_MIXERS
        shift, scale, gate = ada_mod(c, ada_w[i, 0], ada_b[i, 0])
        h = x * scale + shift
        if i % N_MIXERS == 0:
            f = short_conv_mixer(h, conv_w_in[j], conv_w[j], conv_w_out[j])
        else:
            f = diff_attention(h, attn_w_qkv[j], attn_lambda[j], attn_subln_g[j],
                               attn_w_o[j], lambda_init_fn(i))
        x = layer_norm(DEEPNORM_ALPHA * x + gate * f, ln_g[i, 0], ln_b[i, 0])
        shift, scale, gate = ada_mod(c, ada_w[i, 1], ada_b[i, 1])
        h = x * scale + shift
        f = peer_ffn(h, peer_w_q[i], peer_sub_keys[i], peer_u[i], peer_v[i])
        x = layer_norm(DEEPNORM_ALPHA * x + gate * f, ln_g[i, 1], ln_b[i, 1])
    return x


def setup_inputs(seed=0):
    out = dict(first_inputs(seed))
    for name, value in second_inputs(seed + 1).items():
        if name != "x":
            out[name + "_2"] = value
    return out


def reference(
    x, c, positions, cond_w, cond_b, norm_g, ffn_w_gu, ffn_w_down, gla_w_in, gla_w_gate_up,
    gla_b_gate, gla_g_out, gla_w_out, kv_g_in, kv_cond_w, kv_cond_b, mla_w_kv_a, mla_g_kv,
    mla_w_kv_b, mla_w_dq, mla_g_q, mla_w_uq, mla_w_out, c_2, ada_w_2, ada_b_2, ln_g_2, ln_b_2,
    conv_w_in_2, conv_w_2, conv_w_out_2, attn_w_qkv_2, attn_lambda_2, attn_subln_g_2,
    attn_w_o_2, peer_w_q_2, peer_sub_keys_2, peer_u_2, peer_v_2,
):
    x = first_block(
        x, c, positions, cond_w, cond_b, norm_g, ffn_w_gu, ffn_w_down, gla_w_in, gla_w_gate_up,
        gla_b_gate, gla_g_out, gla_w_out, kv_g_in, kv_cond_w, kv_cond_b, mla_w_kv_a, mla_g_kv,
        mla_w_kv_b, mla_w_dq, mla_g_q, mla_w_uq, mla_w_out,
    )
    return second_block(
        x, c_2, ada_w_2, ada_b_2, ln_g_2, ln_b_2, conv_w_in_2, conv_w_2, conv_w_out_2,
        attn_w_qkv_2, attn_lambda_2, attn_subln_g_2, attn_w_o_2, peer_w_q_2, peer_sub_keys_2,
        peer_u_2, peer_v_2,
    )


_drawn_inputs = setup_inputs


def setup_inputs(seed=0):
    import zlib

    import numpy as np

    out = dict(_drawn_inputs(seed))
    spreads = {}
    factors = {'kv_cond_b': 6.726, 'mla_g_q': 3.668, 'attn_subln_g_2': 22.784}
    for name, (base, spread) in spreads.items():
        noise = np.random.default_rng([zlib.crc32(name.encode()), seed]).standard_normal(out[name].shape)
        drawn = base * np.exp(spread * noise) if base else spread * noise
        out[name] = __import__('jax').numpy.asarray(drawn.astype(out[name].dtype))
    for name, factor in factors.items():
        out[name] = (out[name] * factor).astype(out[name].dtype)
    return out
```

```python
from contextlib import ExitStack

import numpy as np

import concourse.bass as bass
from concourse import mybir

F32 = mybir.dt.float32
I32 = mybir.dt.int32
U32 = mybir.dt.uint32
ALU = mybir.AluOpType
ACT = mybir.ActivationFunctionType
AX = mybir.AxisListType.X

P = 128
T = 256
TB = T // P
D = 1024
KD = D // P
HALF = 512
FF = 2816
FT = FF // P
EPS = 1e-6
LN_EPS = 1e-5
GH, GDK, GDV, GRANK, GTAU, CH = 4, 128, 256, 16, 16.0, 64
NCH = T // CH
MH, NOPE, ROPE, VH, KVL, QL = 8, 128, 64, 128, 256, 384
THETA = 10000.0
AH, ADH = 8, 64
PH, PK, NK = 8, 16, 128
NSLOT = PH * PK
ALPHA = 4.0 ** 0.25
LAMBDA_INIT = 0.8 - 0.6 * float(np.exp(-0.3))
NEG = -3.0e38
MISC = 10

RING = 4
ARENA = 14608
MRING = 2
GROUP = 8

STAGES = [("ffn", 0), ("gla", 0), ("ffn", 1), ("kv", 0), ("ffn", 2), ("mla", 0), ("ffn", 3),
          ("conv", 0), ("peer", 0), ("attn", 0), ("peer", 1)]
UNITS = {"ffn": 4 + FT, "gla": 4 + 1 + 2 + 2 + 4 + 4 + 2 + 2 + 2 + 2 + 6 + 4 + 4,
         "kv": 4 + 2 + 2 + 4 + 4, "mla": 4 + 2 + 2 + 4 + 2 + 2 + 3 * 8,
         "conv": 4 + 1 + 12, "peer": 4 + 8 + 1 + 8, "attn": 4 + 12 + 8 * 4 + 4}
LOADS = {"ffn": 11 + 6, "gla": 7 + 2, "kv": 3, "mla": 3 + 2, "conv": 6 + 2, "peer": 4, "attn": 6 + 2}
MOD_ROWS = {"kv": 2}


class Turn:

    def __init__(self):
        self.n = 0

    def next(self, k=1):
        self.n += k
        return self.n


class Stage:
    def __init__(self, n, kind, which, unit, load, mod):
        self.n, self.kind, self.which = n, kind, which
        self.u, self.w, self.m = unit, load, mod
        self.mods = 2 * MOD_ROWS.get(kind, 3)


def plan(upto):
    stages, u, w, m = [], 0, 0, 0
    for n, (kind, which) in enumerate(STAGES[:upto]):
        stages.append(Stage(n, kind, which, u, w, m))
        u += UNITS[kind]
        w += LOADS[kind]
        m += stages[-1].mods
    return stages


def build(nc, a, out, upto=len(STAGES)):
    stages = plan(upto)
    with ExitStack() as ctx:
        _program(nc, ctx, a, out, stages)


def _program(nc, ctx, a, out, stages):
    def sb(name, shape, dt=F32):
        return ctx.enter_context(nc.sbuf_tensor(name, shape, dt))

    def sem(name):
        return ctx.enter_context(nc.semaphore(name))

    ring = sb("ring", [P, RING, 4096])
    mring = sb("mring", [P, MRING, 4, HALF])
    macc = sb("macc", [P, 2, HALF])
    brow = sb("brow", [1, 2, HALF])
    M = sb("M", [P, 2, 3, D])
    x = sb("x", [P, TB, D])
    h = sb("h", [P, TB, D])
    hT = sb("hT", [P, KD, T])
    arena = sb("arena", [P, ARENA])
    ident = sb("ident", [P, P])
    ones = sb("ones", [P, P])
    cvec = sb("cvec", [P, 2, KD])
    cact = sb("cact", [P, 2, KD])
    small = sb("small", [P, 320])
    rope = sb("rope", [P, 2, TB, ROPE // 2])
    tri = sb("tri", [P, P])
    dist = sb("dist", [P, 2 * P])
    gout = sb("gout", [P, 256])
    lamt = sb("lamt", [P, 4 * ADH])
    sums, roots = small[:, 40:42], small[:, 42:44]
    stats = small[:, 128:160]
    lam2, neg_lam = small[:, 2:4], small[:, 4:5]
    eps6, eps5 = small[:, 0:1], small[:, 1:2]
    lnst = small[:, 16:40].rearrange("p (b s n) -> p b s n", b=2, s=2)
    lnag = small[:, 44:48].rearrange("p (b n) -> p b n", b=2)

    def view(off, *dims):
        n = int(np.prod(dims))
        assert off + n <= ARENA
        v = arena[:, off:off + n]
        if len(dims) == 2:
            return v.rearrange("p (a b) -> p a b", a=dims[0])
        if len(dims) == 3:
            return v.rearrange("p (a b c) -> p a b c", a=dims[0], b=dims[1])
        return v

    cb = hT[:, :, 0:P]
    actT = view(0, FT, T)
    sg = view(FT * T, 2, T)
    knT = view(6144, MH, T)
    vmla = view(8192, TB, D)
    krT = view(10240, 2, T)
    g_q, g_k = view(0, GH, T), view(1024, GH, T)
    g_la = view(2048, TB, 512)
    g_eu = view(2048, GH, T)
    g_b = view(3072, GH, T)
    g_tmp = view(3072, TB, 512)
    g_ktok = view(3072, TB, 512)
    g_junk = view(3072, 8, GDV)
    g_eb, g_en = view(4096, GH, T), view(5120, GH, T)
    g_v, g_r = view(6144, TB, D), view(8192, TB, D)
    g_att = view(10240, TB, GH, P)
    g_st = view(0, NCH - 1, GH, GDV)
    g_low = view(11264, T)
    g_wup = view(11520, 512)
    brs = arena[0:1, 12032:12544]
    m_c, m_cT = view(0, TB, QL), view(768, 3, T)
    m_qr, m_qrT = view(1536, TB, 512), view(2560, 4, T)
    m_qnT = view(3584, MH, T)
    m_p = arena[:, 10752:11776].rearrange("p (s h t) -> p s h t", s=2, h=2)
    m_pT = view(11776, 2, 4, P)
    m_t = view(12800, 4, T)
    m_mask = view(13824, 2 * P)
    kv_c, kv_cT = view(0, TB, KVL), view(512, 2, T)
    kv_r = view(1024, TB, P)
    kv_raw = view(1280, TB, KVL + ROPE)
    LN0 = ARENA - 4096
    ln = arena[:, LN0:].rearrange("p (s v n) -> p s v n", s=2, v=2)
    c_gb, c_gc, c_z = view(0, KD, T), view(2048, KD, T), view(4096, KD, T + 2)
    c_w = view(6288, 24)
    a_q, a_v = view(0, KD, T), view(6144, TB, D)
    a_k = arena[:, 2048:6144].rearrange("p (h s t) -> p h s t", h=AH, s=2)
    a_p = hT[:].rearrange("p (s h q) t -> p s h q t", s=2, h=2)
    a_d = view(8192, 2, T)
    a_pT = view(8704, 2, 4, P)
    p_qT = view(0, 16, T)
    p_sc = view(4096, 16, NK)
    p_oh = view(6144, NSLOT, PK)
    p_sk = view(6144, 2, P)
    p_skT = view(8192, 2, P)
    p_sv = view(8448, 16, PK)
    p_si = arena[:, 8704:8960].bitcast(U32).rearrange("p (a b) -> p a b", a=16)
    p_sf = view(8960, 16, PK)
    p_ts = view(9216, PH, PK)
    p_pos = arena[:, 9344:9472].bitcast(U32)
    p_ij = arena[:, 9472:9600].bitcast(U32)
    p_if = view(9600, NSLOT)
    p_e = view(9728, 2, NSLOT)
    p_g = view(9984, TB, NSLOT)
    p_idx = arena[:, 10240:10504].bitcast(U32)
    p_iota = small[:, 48:64]
    p_dots = small[:, 64:80].rearrange("p (s n) -> p s n", s=2)
    p_gel = small[:, 80:96].rearrange("p (s n) -> p s n", s=2)
    p_icur = small[:, 96:112].bitcast(U32).rearrange("p (s n) -> p s n", s=2)
    p_w = small[:, 112:128].rearrange("p (s n) -> p s n", s=2)
    p_diag = sb("p_diag", [P, GROUP, P])
    p_junk = hT[:].rearrange("p (s a) b -> p s (a b)", s=2)
    zeros = sb("zeros", [P, P])
    gains = sb("gains", [P, KVL + QL + 2 * ADH])
    g_kv, g_ql, g_sub = gains[:, 0:KVL], gains[:, KVL:KVL + QL], gains[:, KVL + QL:]
    invf = sb("invf", [P, ROPE // 2])
    cw24 = sb("cw24", [24, P])

    psF = ctx.enter_context(nc.psum_tensor("psF", [P, TB, D], F32))
    psW = [ctx.enter_context(nc.psum_tensor(f"psW{i}", [P, HALF], F32)) for i in range(3)]
    psM = ctx.enter_context(nc.psum_tensor("psM", [P, HALF], F32))

    w_loaded = [sem(f"w_loaded{i}") for i in range(RING)]
    w_used = sem("w_used")
    m_loaded = [sem(f"m_loaded{i}") for i in range(MRING)]
    m_used = sem("m_used")
    b_loaded = [sem(f"b_loaded{i}") for i in range(2)]
    g_loaded = [sem(f"g_loaded{i}") for i in range(2)]
    ln_loaded = [sem(f"ln_loaded{i}") for i in range(2)]
    misc_loaded = sem("misc_loaded")
    c_loaded = sem("c_loaded")
    x_loaded = sem("x_loaded")
    cb_ready = sem("cb_ready")
    keys_loaded = sem("keys_loaded")
    m_reduced = sem("m_reduced")
    m_stored = sem("m_stored")
    unit_full = sem("unit_full")
    unit_stored = sem("unit_stored")
    x_ready = sem("x_ready")
    h_ready = sem("h_ready")
    root_ready = sem("root_ready")
    var_ready = sem("var_ready")
    const_ready = sem("const_ready")
    cact_ready = sem("cact_ready")
    gate_ready = sem("gate_ready")
    act_input_ready = sem("act_input_ready")
    act_result_ready = sem("act_result_ready")
    yT_ready = sem("yT_ready")
    att_ready = sem("att_ready")
    dve_step = sem("dve_step")
    act_step = sem("act_step")
    pool_step = sem("pool_step")
    state_ready = sem("state_ready")
    idx_ready = sem("idx_ready")
    u_loaded = [sem(f"u_loaded{i}") for i in range(GROUP)]
    v_loaded = [sem(f"v_loaded{i}") for i in range(GROUP)]
    dot_done = sem("dot_done")
    v_used = sem("v_used")
    AHEAD = 1
    CHOSEN = 4
    u_free = sem("u_free")
    v_free = sem("v_free")
    w_ready = sem("w_ready")
    gelu_ready = sem("gelu_ready")
    diag_ready = sem("diag_ready")
    stored = sem("stored")

    last = stages[-1]

    def row_u(s):
        return ring[:, s // 4, (s % 4) * D:(s % 4 + 1) * D]

    def row_v(s):
        return ring[:, 2 + s // 4, (s % 4) * D:(s % 4 + 1) * D]

    def cols(w, c0, n):
        return w.rearrange("(k p) n -> p k n", p=P)[:, :, c0:c0 + n]

    def slot(i, k, n):
        return ring[:, i % RING, 0:k * n].rearrange("p (k n) -> p k n", k=k)

    def slot_kv(i, q):
        return ring[:, i % RING, 0:2048].rearrange("p (k q n) -> p k q n", k=2, q=2)[:, :, q, :]

    def stage_loads(st):
        i = st.w
        if st.kind == "ffn":
            gu = a["ffn_w_gu"][st.which // 2, st.which % 2]
            dn = a["ffn_w_down"][st.which // 2, st.which % 2].rearrange("(k p) n -> p k n", p=P)
            for s in range(11):
                yield [(slot(i, KD, HALF)[:, :, 0:256], cols(gu, 256 * s, 256)),
                       (slot(i, KD, HALF)[:, :, 256:512], cols(gu, FF + 256 * s, 256))], st.u + 5 + 2 * s
                i += 1
            for s in range(6):
                k = min(4, FT - 4 * s)
                yield [(slot(i, k, D), dn[:, 4 * s:4 * s + k, :])], None
                i += 1
        elif st.kind == "gla":
            w = a["gla_w_in"][0]
            yield [(slot(i, KD, GRANK), cols(w, 2048, GRANK))], st.u + 4
            for j, (c0, u) in enumerate(((1024, 6), (1536, 10), (2064, 12), (2576, 14), (0, 18), (512, 20))):
                yield [(slot(i + 1 + j, KD, HALF), cols(w, c0, HALF))], st.u + u
            wo = a["gla_w_out"][0].rearrange("(k p) n -> p k n", p=P)
            for j in range(2):
                yield [(slot(i + 7 + j, 4, D), wo[:, 4 * j:4 * j + 4, :])], None
        elif st.kind == "kv":
            yield [(slot(i, KD, KVL + ROPE), cols(a["mla_w_kv_a"], 0, KVL + ROPE))], st.u + 5
            w = a["mla_w_kv_b"].rearrange("(k p) (g h q c) -> g q p k h c", p=P, g=2, h=4, q=2)
            for j in range(2):
                yield [(slot_kv(i + 1 + j, q)[:, k, :].rearrange("p (h c) -> p h c", c=P), w[j, q, :, k])
                       for q in range(2) for k in range(2)], st.u + 11 + 4 * j
        elif st.kind == "mla":
            yield [(slot(i, KD, QL), cols(a["mla_w_dq"][0], 0, QL))], st.u + 5
            w = a["mla_w_uq"][0].rearrange("(k p) (h c) -> p k h c", p=P, c=NOPE + ROPE)
            yield [(slot(i + 1, 3, D)[:, k, :].rearrange("p (h c) -> p h c", c=NOPE), w[:, k, :, 0:NOPE])
                   for k in range(3)], st.u + 11
            yield [(slot(i + 2, 3, 512)[:, k, :].rearrange("p (h c) -> p h c", c=ROPE), w[:, k, :, NOPE:])
                   for k in range(3)], st.u + 13
            wo = a["mla_w_out"][0].rearrange("(k p) n -> p k n", p=P)
            for j in range(2):
                yield [(slot(i + 3 + j, 4, D), wo[:, 4 * j:4 * j + 4, :])], None
        elif st.kind in ("conv", "attn"):
            w, wo = ((a["conv_w_in_2"][0], a["conv_w_out_2"][0]) if st.kind == "conv"
                     else (a["attn_w_qkv_2"][0], a["attn_w_o_2"][0]))
            wo = wo.rearrange("(k p) n -> p k n", p=P)
            u0 = st.u + (5 if st.kind == "conv" else 4)
            for j in range(6):
                yield [(slot(i + j, KD, HALF), cols(w, HALF * j, HALF))], u0 + 2 * j + 1
            for j in range(2):
                yield [(slot(i + 6 + j, 4, D), wo[:, 4 * j:4 * j + 4, :])], None
        else:
            for j in range(4):
                yield [(slot(i + j, KD, HALF), cols(a["peer_w_q_2"][st.which], HALF * j, HALF))], st.u + 13 + j

    loads = [l for st in stages for l in stage_loads(st)]
    assert len(loads) == last.w + LOADS[last.kind]
    landed, so_far = [], [0] * RING
    for i, l in enumerate(loads):
        so_far[i % RING] += 16 * len(l[0])
        landed.append(so_far[i % RING])

    outputs = [sum(l[1] is None for l in loads[:i + 1]) for i in range(len(loads))]

    def x_count(n):
        return TB * (1 + sum(s.kind != "kv" for s in stages[:n]))

    def h_count(n):
        return TB * sum(2 if s.kind in ("gla", "attn") else 1 for s in stages[:n])

    def peers(n):
        return sum(s.kind == "peer" for s in stages[:n])

    def slot_free(eng, i):
        if loads[i][1] is None:
            eng.wait_ge(w_used, outputs[i])
        else:
            eng.wait_ge(unit_full, loads[i][1] + 1)

    def output_done(eng, st):
        if st.kind == "peer":
            eng.wait_ge(v_used, AHEAD + TB * NSLOT * peers(st.n + 1))
        else:
            eng.wait_ge(w_used, outputs[st.w + LOADS[st.kind] - 1])

    def mod_source(st):
        n = st.n
        if st.kind == "kv":
            return a["kv_cond_w"], a["kv_cond_b"], 0
        if n < 7:
            layer, s = (0, n) if n < 3 else (1, n - 4)
            return (a["cond_w"][layer][:, 3 * D * s:3 * D * (s + 1)],
                    a["cond_b"][layer][3 * D * s:3 * D * (s + 1)], 0)
        i, m = divmod(n - 7, 2)
        return a["ada_w_2"][i, m], a["ada_b_2"][i, m], 1

    pieces = [(st, j) for st in stages for j in range(st.mods)]

    def modulation_weights(eng, i):
        st, j = pieces[i // 2]
        w = mod_source(st)[0].rearrange("(p k) n -> p k n", p=P)
        q = i % 2
        eng.dma_start(mring[:, i % MRING], w[:, 4 * q:4 * q + 4, HALF * j:HALF * (j + 1)])\
            .then_inc(m_loaded[i % MRING], 16)

    def bias_row(eng, n):
        st, j = pieces[n]
        b = mod_source(st)[1].rearrange("(o n) -> o n", o=1)
        eng.dma_start(brow[:, n % 2, :], b[:, HALF * j:HALF * (j + 1)]).then_inc(b_loaded[n % 2], 16)

    def gains(eng, st):
        par = st.n % 2
        if st.n >= 2:
            eng.wait_ge(x_ready, x_count(st.n - 1))
            if stages[st.n - 2].kind == "kv":
                eng.wait_ge(h_ready, h_count(st.n - 1))
        if st.n >= 7:
            i, m = divmod(st.n - 7, 2)
            for j, name in enumerate(("ln_g_2", "ln_b_2")):
                eng.dma_start(ln[:, par, j, :], a[name][i, m:m + 1, :].to_broadcast([P, D]))\
                    .then_inc(ln_loaded[par], 16)
        elif st.kind == "kv":
            eng.dma_start(M[:, par, 1, :], a["kv_g_in"].rearrange("(o n) -> o n", o=1).to_broadcast([P, D]))\
                .then_inc(g_loaded[par], 32)
        else:
            layer, s = (0, st.n) if st.n < 3 else (1, st.n - 4)
            for j in range(2):
                eng.dma_start(M[:, par, 1 + j, :], a["norm_g"][layer, s, j:j + 1, :].to_broadcast([P, D]))\
                    .then_inc(g_loaded[par], 16)

    block = ctx.enter_context(nc.Block())

    @block.sync
    def _(sp):
        def fill(i):
            if i >= RING:
                slot_free(sp, i - RING)
            for d, s in loads[i][0]:
                sp.dma_start(d, s).then_inc(w_loaded[i % RING], 16)

        for i, name in enumerate(("c", "c_2")):
            sp.dma_start(cvec[:, i, :], a[name].rearrange("o (p k) -> p (o k)", p=P)).then_inc(c_loaded, 16)
        sp.dma_start(x[:], a["x"].rearrange("o (b p) n -> p (o b) n", p=P)).then_inc(x_loaded, 16)
        sp.dma_start(small[:, 8:10].bitcast(I32), a["positions"].rearrange("o (b p) -> p (o b)", p=P),
                       allow_slow_non_contiguous=True).then_inc(misc_loaded, 16)
        sp.dma_start(g_wup[0:GRANK, :], a["gla_w_gate_up"][0]).then_inc(misc_loaded, 16)
        sp.dma_start(brs, a["gla_b_gate"]).then_inc(misc_loaded, 16)
        sp.dma_start(gout[:], a["gla_g_out"].to_broadcast([P, GDV])).then_inc(misc_loaded, 16)
        sp.dma_start(lamt[:], a["attn_lambda_2"].rearrange("o a b -> o (a b)").to_broadcast([P, 4 * ADH]))\
            .then_inc(misc_loaded, 16)

        for t, name in ((g_kv, "mla_g_kv"), (invf[:], "inv_freq")):
            sp.dma_start(t, a[name].rearrange("(o n) -> o n", o=1).to_broadcast([P, t.shape[1]]))\
                .then_inc(misc_loaded, 16)
        for t, name in ((g_ql, "mla_g_q"), (g_sub, "attn_subln_g_2")):
            sp.dma_start(t, a[name].to_broadcast([P, t.shape[1]])).then_inc(misc_loaded, 16)
        sp.dma_start(cw24[:], a["conv_w_2"].rearrange("o w (k p) -> (o w k) p", p=P)).then_inc(misc_loaded, 16)
        sp.wait_ge(m_used, 2 * stages[0].mods - MRING)
        for st in stages:
            for j in range(LOADS[st.kind]):
                if j == 0 and st.n and stages[st.n - 1].kind == "peer":
                    sp.wait_ge(dot_done, AHEAD + peers(st.n) * TB * NSLOT)
                    sp.wait_ge(v_used, AHEAD + peers(st.n) * TB * NSLOT)
                fill(st.w + j)
        sp.wait_ge(x_ready, x_count(len(stages)))
        sp.dma_start(out.rearrange("o (b p) n -> p (o b) n", p=P), x[:]).then_inc(stored, 16)
        sp.wait_ge(stored, 16)

    def pool_peer(pool, st):
        tables = [a[name].rearrange("l e n -> (l e) n") for name in ("peer_u_2", "peer_v_2")]
        for b in range(TB):
            g0 = (st.which * TB + b) * NSLOT
            with pool.Fori(0, NSLOT // (2 * GROUP)) as it:
                for q in range(2):
                    done = it * (2 * GROUP) + (g0 + q * GROUP + AHEAD)
                    pool.wait_ge(idx_ready, it * 2 + (g0 // GROUP + q + 1 + st.which))
                    pool.wait_ge(dot_done, done)
                    pool.sem_inc(u_free, 1)
                    slot_free(pool, st.w + 3)
                    for s in range(GROUP):
                        pool.indirect_dma_start(
                            out=row_u(s), out_offset=None, in_=tables[0],
                            in_offset=bass.IndirectOffsetOnAxis(ap=p_icur[:, q, s:s + 1], axis=0),
                        ).then_inc(u_loaded[s], 16)
                    pool.wait_ge(v_used, done)
                    pool.sem_inc(v_free, 1)
                    slot_free(pool, st.w + 3)
                    for s in range(GROUP):
                        pool.indirect_dma_start(
                            out=row_v(s), out_offset=None, in_=tables[1],
                            in_offset=bass.IndirectOffsetOnAxis(ap=p_icur[:, q, s:s + 1], axis=0),
                        ).then_inc(v_loaded[s], 16)

    @block.gpsimd
    def _(pool):
        chain = Turn()

        def link(ins):
            ins.then_inc(pool_step, 1)
            pool.wait_ge(pool_step, chain.next())

        def first_modulation(n):
            if n >= 2:
                pool.wait_ge(m_reduced, n - 1)
            bias_row(pool, n)
            for i in (2 * n, 2 * n + 1):
                if i >= MRING:
                    pool.wait_ge(m_used, i - MRING + 1)
                modulation_weights(pool, i)

        first_modulation(0)
        link(pool.memset(ident[:], 0.0))
        pool.memset(ones[:], 1.0)
        pool.memset(zeros[:], 0.0)
        pool.memset(eps6, EPS)
        pool.memset(eps5, LN_EPS)
        link(pool.affine_select(out=ident[:], in_=ident[:], compare_op=ALU.not_equal, fill=1.0, base=0,
                                pattern=[[-1, P]], channel_multiplier=1))
        link(pool.memset(tri[:], 1.0))
        link(pool.affine_select(out=tri[:], in_=tri[:], compare_op=ALU.is_ge, fill=0.0, base=0,
                                pattern=[[1, P]], channel_multiplier=-1))
        link(pool.memset(tri[0:CH, CH:], 0.0))
        link(pool.iota(dist[:].bitcast(I32), [[-1, 2 * P]], base=P, channel_multiplier=1))
        link(pool.tensor_copy(dist[:], dist[:].bitcast(I32)))
        link(pool.affine_select(out=dist[:], in_=dist[:], compare_op=ALU.is_ge, fill=-NEG, base=P,
                                pattern=[[-1, 2 * P]], channel_multiplier=1))
        link(pool.iota(p_iota.bitcast(I32), [[1, PK]], base=0, channel_multiplier=0))
        pool.tensor_copy(p_iota, p_iota.bitcast(I32)).then_inc(const_ready, 1)
        for n in range(1, stages[0].mods):
            first_modulation(n)
            if n == 1:
                gains(pool, stages[0])

        def load(i):
            pool.wait_ge(m_used, i - MRING + 1)
            modulation_weights(pool, i)

        def modulation(st):
            for j in range(st.mods):
                n = st.m + j
                pool.wait_ge(m_reduced, n - 1)
                bias_row(pool, n)
                acc = macc[:, n % 2, :]
                for q in range(2):
                    i = 2 * n + q
                    pool.wait_ge(m_loaded[i % MRING], 16 * (i // MRING + 1))
                    w, c = mring[:, i % MRING], cact[:, int(st.n >= 7), 4 * q:4 * q + 4]
                    link(pool.tensor_tensor(w, w, c.unsqueeze(2).to_broadcast([P, 4, HALF]), ALU.mult))
                    link(pool.tensor_tensor(w[:, 0:2], w[:, 0:2], w[:, 2:4], ALU.add))
                    if q:
                        link(pool.tensor_tensor(acc, acc, w[:, 0, :], ALU.add))
                        ins = pool.tensor_tensor(acc, acc, w[:, 1, :], ALU.add)
                    else:
                        ins = pool.tensor_tensor(acc, w[:, 0, :], w[:, 1, :], ALU.add)
                    ins.then_inc(m_used, 1)
                    pool.wait_ge(m_used, i + 1)
                    if i + MRING < 2 * len(pieces):
                        load(i + MRING)
                if j == 1:
                    gains(pool, st)

        pool.wait_ge(cact_ready, 1)
        if len(stages) > 1:
            for i in range(MRING):
                load(2 * stages[1].m + i)
        for st in stages:
            if st.kind == "peer":
                pool.wait_ge(x_ready, x_count(st.n))
                pool.dma_start(p_sk, a["peer_sub_keys_2"][st.which].rearrange("s n d -> n s d"))\
                    .then_inc(keys_loaded, 16)
            if st.n + 1 < len(stages):
                modulation(stages[st.n + 1])
            if st.kind == "peer":
                pool_peer(pool, st)

    @block.tensor
    def _(pe):
        t_h, t_sum, t_dve = Turn(), Turn(), Turn()

        def open_unit(u):
            if u >= 3:
                pe.wait_ge(unit_stored, u - 2)
            return psW[u % 3]

        def have(u):
            pe.wait_ge(unit_stored, u + 1)

        def arrived(i):
            pe.wait_ge(w_loaded[i % RING], landed[i])

        def sum_row(n):
            if n >= 1:
                pe.wait_ge(m_stored, n)
            pe.wait_ge(m_used, 2 * n + 2)
            pe.matmul(psM[:], ones[:], macc[:, n % 2, :], start=True, stop=False)
            add_bias(n)

        def add_bias(n):
            pe.wait_ge(b_loaded[n % 2], 16 * (n // 2 + 1))
            pe.matmul(psM[:], ones[0:1, :], brow[:, n % 2, :], start=False, stop=True).then_inc(m_reduced, 1)

        def hook(st, q, of):
            if st.n + 1 < len(stages):
                nx = stages[st.n + 1]
                for j in range(nx.mods * max(q - 1, 0) // of, nx.mods * q // of):
                    sum_row(nx.m + j)

        def transposes(u):
            for b in range(TB):
                pe.wait_ge(h_ready, t_h.next())
                for g in range(2):
                    ps = open_unit(u)
                    for j in range(4):
                        ins = pe.transpose(ps[:, j * P:(j + 1) * P], h[:, b, (4 * g + j) * P:(4 * g + j + 1) * P],
                                           ident[:])
                    ins.then_inc(unit_full, 1)
                    u += 1
            return u

        def by_weights(u, w, rhs, kd, tiles, c0=0):
            for t in range(0, tiles, 2):
                ps = open_unit(u)
                for j in range(2):
                    for k in range(kd):
                        ins = pe.matmul(ps[:, j * T:(j + 1) * T], w[:, k, c0 + (t + j) * P:c0 + (t + j + 1) * P],
                                        rhs[:, k, :], start=(k == 0), stop=(k == kd - 1))
                ins.then_inc(unit_full, 1)
                u += 1
            return u

        def by_tokens(u, w, lhs, kd, n):
            for b in range(TB):
                ps = open_unit(u)
                for k in range(kd):
                    ins = pe.matmul(ps[:, 0:n], lhs[:, k, b * P:(b + 1) * P], w[:, k, 0:n],
                                    start=(k == 0), stop=(k == kd - 1))
                ins.then_inc(unit_full, 1)
                u += 1
            return u

        def project(st, i, lhs, kt, of):
            for g in range(0, kt, 4):
                arrived(i)
                n = min(4, kt - g)
                w = slot(i, n, D)
                for k in range(n):
                    for b in range(TB):
                        for f in range(2):
                            ins = pe.matmul(psF[:, b, f * HALF:(f + 1) * HALF], lhs[:, g + k, b * P:(b + 1) * P],
                                            w[:, k, f * HALF:(f + 1) * HALF], start=(g + k == 0),
                                            stop=(g + k == kt - 1))
                ins.then_inc(w_used, 1)
                i += 1
                if g == 0:
                    hook(st, of, of)

        def ffn(st):
            u = transposes(st.u)
            have(u - 1)
            for s in range(11):
                i = st.w + s
                arrived(i)
                w = slot(i, KD, HALF)
                for c in range(2):
                    ps = open_unit(u)
                    for part in range(2):
                        for k in range(KD):
                            ins = pe.matmul(ps[:, part * T:(part + 1) * T],
                                            w[:, k, part * 256 + c * P:part * 256 + (c + 1) * P], hT[:, k, :],
                                            start=(k == 0), stop=(k == KD - 1))
                    ins.then_inc(unit_full, 1)
                    u += 1
                hook(st, s, 11)
            have(u - 1)
            project(st, st.w + 11, actT, FT, 11)

        def gla(st):
            u = transposes(st.u)
            i = st.w
            have(u - 1)
            arrived(i)
            w = slot(i, KD, GRANK)
            ps = open_unit(u)
            for k in range(KD):
                ins = pe.matmul(ps[0:GRANK, 0:T], w[:, k, :], hT[:, k, :], start=(k == 0), stop=(k == KD - 1))
            ins.then_inc(unit_full, 1)
            u += 1
            for j in range(4):
                arrived(i + 1 + j)
                u = by_tokens(u, slot(i + 1 + j, KD, HALF), hT, KD, HALF)
                if j == 0:
                    for b in range(TB):
                        ps = open_unit(u)
                        pe.matmul(ps[:], g_low[0:GRANK, b * P:(b + 1) * P], g_wup[0:GRANK, :], start=True, stop=False)
                        pe.matmul(ps[:], ones[0:1, :], brs, start=False, stop=True).then_inc(unit_full, 1)
                        u += 1
                hook(st, j, 6)
            pe.wait_ge(state_ready, 1)
            for g in range(2):
                ps = open_unit(u)
                for hh in range(2):
                    for b in range(TB):
                        ins = pe.matmul(ps[:, hh * T + b * P:hh * T + (b + 1) * P],
                                        g_la[:, b, (2 * g + hh) * P:(2 * g + hh + 1) * P], tri[:],
                                        start=True, stop=True)
                ins.then_inc(unit_full, 1)
                u += 1
            for j in range(2):
                arrived(i + 5 + j)
                u = by_weights(u, slot(i + 5 + j, KD, HALF), hT, KD, 4)
                hook(st, 4 + j, 6)
            pe.wait_ge(state_ready, 2)
            for b in range(TB):
                ps = open_unit(u)
                for hh in range(GH):
                    ins = pe.transpose(ps[:, hh * P:(hh + 1) * P], g_eu[:, hh, b * P:(b + 1) * P], ident[:])
                ins.then_inc(unit_full, 1)
                u += 1
            for b in range(TB):
                ps = open_unit(u)
                for hh in range(GH):
                    ins = pe.matmul(ps[:, hh * P:(hh + 1) * P], g_en[:, hh, b * P:(b + 1) * P],
                                    g_eb[:, hh, b * P:(b + 1) * P], start=True, stop=True)
                ins.then_inc(unit_full, 1)
                u += 1
            have(u - 3)
            for n in range(NCH - 1):
                b, c = divmod(n, 2)
                for g in range(2):
                    ps = open_unit(u)
                    for hh in range(2):
                        hd = 2 * g + hh
                        ins = pe.matmul(ps[:, hh * GDV:(hh + 1) * GDV],
                                        g_ktok[c * CH:(c + 1) * CH, b, hd * P:(hd + 1) * P],
                                        g_v[c * CH:(c + 1) * CH, b, hd * GDV:(hd + 1) * GDV], start=True, stop=True)
                    ins.then_inc(unit_full, 1)
                    u += 1
            have(u - 1)
            for b in range(TB):
                for g in range(2):
                    ps = open_unit(u)
                    for hh in range(2):
                        hd = 2 * g + hh
                        o = ps[:, hh * GDV:(hh + 1) * GDV]
                        ins = pe.matmul(o, g_att[:, b, hd, :], g_v[:, b, hd * GDV:(hd + 1) * GDV],
                                        start=True, stop=False, skip_group_check=True)
                        for c in range(2):
                            n = 2 * b + c
                            if n:
                                ins = pe.matmul(o[c * CH:(c + 1) * CH, :],
                                                g_eb[:, hd, n * CH:(n + 1) * CH], g_st[:, n - 1, hd, :],
                                                start=False, stop=True, skip_group_check=True)
                    ins.then_inc(unit_full, 1)
                    u += 1
            u = transposes(u)
            have(u - 1)
            project(st, i + 7, hT, KD, 6)
            assert u == st.u + UNITS["gla"]

        def kv(st):
            u = transposes(st.u)
            i = st.w
            have(u - 1)
            arrived(i)
            u = by_tokens(u, slot(i, KD, KVL + ROPE), hT, KD, KVL + ROPE)
            for b in range(TB):
                hook(st, b, TB + 1)
                pe.wait_ge(yT_ready, t_dve.next())
                ps = open_unit(u)
                for j in range(2):
                    pe.transpose(ps[:, j * P:(j + 1) * P], kv_c[:, b, j * P:(j + 1) * P], ident[:])
                pe.transpose(ps[:, 2 * P:3 * P], kv_r[:, b, :], ident[:]).then_inc(unit_full, 1)
                u += 1
            have(u - 1)
            hook(st, TB, TB + 1)
            for j in range(2):
                arrived(i + 1 + j)
                u = by_weights(u, slot_kv(i + 1 + j, 0), kv_cT, 2, 4)
                u = by_tokens(u, slot_kv(i + 1 + j, 1), kv_cT, 2, HALF)
            hook(st, TB + 1, TB + 1)

        def mla(st):
            u = transposes(st.u)
            i = st.w
            have(u - 1)
            arrived(i)
            u = by_tokens(u, slot(i, KD, QL), hT, KD, QL)
            hook(st, 0, 3)
            for b in range(TB):
                pe.wait_ge(yT_ready, t_dve.next())
                ps = open_unit(u)
                for j in range(3):
                    ins = pe.transpose(ps[:, j * P:(j + 1) * P], m_c[:, b, j * P:(j + 1) * P], ident[:])
                ins.then_inc(unit_full, 1)
                u += 1
            have(u - 1)
            arrived(i + 1)
            u = by_weights(u, slot(i + 1, 3, D), m_cT, 3, 8)
            hook(st, 1, 3)
            arrived(i + 2)
            u = by_tokens(u, slot(i + 2, 3, 512), m_cT, 3, 512)
            hook(st, 2, 3)
            for b in range(TB):
                pe.wait_ge(yT_ready, t_dve.next())
                ps = open_unit(u)
                for j in range(4):
                    ins = pe.transpose(ps[:, j * P:(j + 1) * P], m_qr[:, b, j * P:(j + 1) * P], ident[:])
                ins.then_inc(unit_full, 1)
                u += 1
            have(u - 1)
            steps = [(b, g) for b in range(TB) for g in range(4)]

            def score(u, b, g):
                n = (b + 1) * P
                ps = open_unit(u)
                for hh in range(2):
                    hd = 2 * g + hh
                    pe.matmul(ps[:, hh * T:hh * T + n], m_qnT[:, hd, b * P:(b + 1) * P], knT[:, hd, 0:n],
                              start=True, stop=False)
                    ins = pe.matmul(ps[:, hh * T:hh * T + n], m_qrT[:, g, b * P:(b + 1) * P], krT[:, hh, 0:n],
                                    start=False, stop=True)
                ins.then_inc(unit_full, 1)

            def turn(u, s, b):
                pe.wait_ge(att_ready, t_sum.next())
                ps = open_unit(u)
                for hh in range(2):
                    for kb in range(b + 1):
                        ins = pe.transpose(ps[:, (2 * hh + kb) * P:(2 * hh + kb + 1) * P],
                                           m_p[:, s % 2, hh, kb * P:(kb + 1) * P], ident[:])
                ins.then_inc(unit_full, 1)

            def value(u, s, b, g):
                have(u - 1)
                ps = open_unit(u)
                for hh in range(2):
                    hd = 2 * g + hh
                    for kb in range(b + 1):
                        ins = pe.matmul(ps[:, hh * P:(hh + 1) * P], vmla[:, kb, hd * P:(hd + 1) * P],
                                        m_pT[:, s % 2, 2 * hh + kb, :], start=(kb == 0), stop=(kb == b))
                ins.then_inc(unit_full, 1)

            score(u, *steps[0])
            u += 1
            for s, (b, g) in enumerate(steps):
                if s + 1 < len(steps):
                    score(u, *steps[s + 1])
                    u += 1
                turn(u, s, b)
                value(u + 1, s, b, g)
                u += 2
            have(u - 1)
            project(st, i + 3, hT, KD, 3)

        def conv(st):
            u = transposes(st.u)
            i = st.w
            have(u - 1)
            ps = open_unit(u)
            pe.transpose(ps[:, 0:24], cw24[:], ident[0:24, 0:24]).then_inc(unit_full, 1)
            u += 1
            for j in range(6):
                arrived(i + j)
                u = by_weights(u, slot(i + j, KD, HALF), hT, KD, 4)
                hook(st, j, 6)
            pe.wait_ge(yT_ready, t_dve.next())
            project(st, i + 6, c_gc, KD, 6)

        def attn(st):
            u = transposes(st.u)
            i = st.w
            have(u - 1)
            for j in range(6):
                arrived(i + j)
                if j < 4:
                    u = by_weights(u, slot(i + j, KD, HALF), hT, KD, 4)
                else:
                    u = by_tokens(u, slot(i + j, KD, HALF), hT, KD, HALF)
                hook(st, j, 6)
            have(u - 1)

            def score(u, s):
                b, g = divmod(s, 4)
                n = (b + 1) * P
                for hh in range(2):
                    hd = 2 * g + hh
                    ps = open_unit(u)
                    for part in range(2):
                        ins = pe.matmul(ps[:, part * T:part * T + n], a_q[:, hd, b * P:(b + 1) * P],
                                        a_k[:, hd, part, 0:n], start=True, stop=True)
                    ins.then_inc(unit_full, 1)
                    u += 1
                return u

            u = score(u, 0)
            for s in range(8):
                b, g = divmod(s, 4)
                if s + 1 < 8:
                    u = score(u, s + 1)
                pe.wait_ge(att_ready, t_sum.next())
                ps = open_unit(u)
                for hh in range(2):
                    for kb in range(b + 1):
                        ins = pe.transpose(ps[:, (2 * hh + kb) * P:(2 * hh + kb + 1) * P],
                                           a_p[:, s % 2, hh, 0, kb * P:(kb + 1) * P], ident[:])
                ins.then_inc(unit_full, 1)
                have(u)
                u += 1
                ps = open_unit(u)
                for hh in range(2):
                    hd = 2 * g + hh
                    for kb in range(b + 1):
                        ins = pe.matmul(ps[:, hh * P:(hh + 1) * P], a_pT[:, s % 2, 2 * hh + kb, :],
                                        a_v[:, kb, hd * P:(hd + 1) * P], start=(kb == 0), stop=(kb == b))
                ins.then_inc(unit_full, 1)
                u += 1
            u = transposes(u)
            have(u - 1)
            project(st, i + 6, hT, KD, 6)

        def peer(st):
            u = transposes(st.u)
            i = st.w
            have(u - 1)

            def queries(u, j, b):
                ps, w = open_unit(u), slot(i + j, KD, HALF)
                for t in range(4):
                    for k in range(KD):
                        ins = pe.matmul(ps[:, t * P:(t + 1) * P], w[:, k, t * P:(t + 1) * P],
                                        hT[:, k, b * P:(b + 1) * P], start=(k == 0), stop=(k == KD - 1))
                ins.then_inc(unit_full, 1)
                return u + 1

            def scores(u, b):
                have(u - 1)
                for g in range(4):
                    ps = open_unit(u)
                    for j in range(4):
                        ins = pe.matmul(ps[:, j * P:(j + 1) * P], p_qT[:, 4 * g + j, b * P:(b + 1) * P],
                                        p_skT[:, j % 2, :], start=True, stop=True)
                    ins.then_inc(unit_full, 1)
                    u += 1
                return u

            for j in range(4):
                arrived(i + j)
                u = queries(u, j, 0)
                hook(st, j, 4)
            pe.wait_ge(keys_loaded, 16 * (st.which + 1))
            ps = open_unit(u)
            for j in range(2):
                ins = pe.transpose(ps[:, j * P:(j + 1) * P], p_sk[:, j, :], ident[:])
            ins.then_inc(unit_full, 1)
            u = scores(u + 1, 0)
            for j in range(4):
                u = queries(u, j, 1)
                if j == 0:
                    hook(st, 4, 4)
            u = scores(u, 1)
            assert u == st.u + UNITS["peer"]
            for b in range(TB):
                g0 = (st.which * TB + b) * NSLOT
                for f in range(2):
                    pe.matmul(psF[:, b, f * HALF:(f + 1) * HALF], zeros[:], h[:, b, f * HALF:(f + 1) * HALF],
                              start=True, stop=False, skip_group_check=True)
                with pe.Fori(0, NSLOT // (2 * GROUP)) as it:
                    for q in range(2):
                        for s in range(GROUP):
                            pe.wait_ge(v_loaded[s], it * 32 + (g0 // GROUP + q + 1) * 16)
                            pe.wait_ge(diag_ready, it * (2 * GROUP) + (g0 + q * GROUP + s + 1))
                            for f in range(2):
                                ins = pe.matmul(psF[:, b, f * HALF:(f + 1) * HALF], p_diag[:, s, :],
                                                row_v(s)[:, f * HALF:(f + 1) * HALF],
                                                start=False, stop=(s == GROUP - 1), skip_group_check=True)
                            ins.then_inc(v_used, 1)

        pe.sem_inc(v_used, AHEAD)
        pe.wait_ge(const_ready, 1)
        pe.wait_ge(cb_ready, 1)
        for n in range(stages[0].mods):
            if n >= 1:
                pe.wait_ge(m_stored, n)
            for i in (2 * n, 2 * n + 1):
                pe.wait_ge(m_loaded[i % MRING], 16 * (i // MRING + 1))
                for k in range(4):
                    ins = pe.matmul(psM[:], cb[:, 4 * (i % 2) + k, :], mring[:, i % MRING, k, :],
                                    start=(i % 2 == k == 0), stop=False)
                ins.then_inc(m_used, 1)
            add_bias(n)
        table = {"ffn": ffn, "gla": gla, "kv": kv, "mla": mla, "conv": conv, "attn": attn, "peer": peer}
        for st in stages:
            table[st.kind](st)

    @block.scalar
    def _(act):
        t_step, t_in, t_var = Turn(), Turn(), Turn()

        def link(ins):
            ins.then_inc(act_step, 1)
            act.wait_ge(act_step, t_step.next())

        def full(u):
            act.wait_ge(unit_full, u + 1)

        def have(u):
            act.wait_ge(unit_stored, u + 1)

        def root_mean_square(st, src, b):
            link(act.activation(h[:, b, :], src, ACT.Square, scale=D ** -0.5, accum_out=sums[:, b:b + 1]))
            act.activation(roots[:, b:b + 1], sums[:, b:b + 1], ACT.Sqrt, bias=eps6).then_inc(root_ready, 1)

        def roots_of(src, acc, parts, width, junk):
            for j in range(parts):
                ins = act.activation(junk(j), src(j), ACT.Square, scale=width ** -0.5, accum_out=acc[:, j:j + 1])
            link(ins)
            act.activation(acc[:, 0:parts], acc[:, 0:parts], ACT.Sqrt, bias=eps6).then_inc(act_result_ready, 1)

        def ffn(st):
            u = st.u + 4
            for j in range(FT):
                full(u + j)
                if j >= 2:
                    have(u + j - 2)
                act.activation(sg[:, j % 2, :], psW[(u + j) % 3][:, 0:T], ACT.Silu).then_inc(gate_ready, 1)

        def gla(st):
            for b in range(TB):
                have(st.u + 7 + b)
                link(act.activation(g_tmp[:, b, :], g_la[:, b, :], ACT.Abs))
                link(act.activation(g_tmp[:, b, :], g_tmp[:, b, :], ACT.Exp, scale=-1.0))
                act.activation(g_tmp[:, b, :], g_tmp[:, b, :], ACT.Ln, bias=ones[:, 0:1]).then_inc(act_result_ready, 1)
            have(st.u + 14)
            act.activation(g_r, g_r, ACT.Silu).then_inc(act_result_ready, 1)
            have(st.u + 16)
            act.activation(g_eb, g_b, ACT.Exp).then_inc(act_result_ready, 1)
            act.activation(g_en, g_b, ACT.Exp, scale=-1.0).then_inc(act_result_ready, 1)
            for hh in range(GH):
                for n in range(NCH):
                    e = (n + 1) * CH
                    ins = act.activation(g_eu[:, hh, e - CH:e], g_b[:, hh, e - CH:e], ACT.Exp, scale=-1.0,
                                         bias=g_b[:, hh, e - 1:e])
            ins.then_inc(act_result_ready, 1)
            have(st.u + 34)
            roots_of(lambda j: h[:, j // 4, (j % 4) * GDV:(j % 4 + 1) * GDV], stats, 8, GDV,
                     lambda j: g_junk[:, j, :])

        def kv(st):
            for b in range(TB):
                have(st.u + 4 + b)
                roots_of(lambda j: kv_raw[:, b, 0:KVL], stats[:, b:b + 1], 1, KVL,
                         lambda j: h[:, b, 0:KVL])

        def mla(st):
            for b in range(TB):
                have(st.u + 4 + b)
                roots_of(lambda j: m_c[:, b, :], stats[:, b:b + 1], 1, QL,
                         lambda j: h[:, b, 0:QL])
            for s in range(8):
                n = (s // 4 + 1) * P
                act.wait_ge(act_input_ready, t_in.next())
                for hh in range(2):
                    ins = act.activation(m_p[:, s % 2, hh, 0:n], m_p[:, s % 2, hh, 0:n], ACT.Exp,
                                         bias=stats[:, 8 + 4 * (s % 2) + hh:9 + 4 * (s % 2) + hh],
                                         accum_out=stats[:, 10 + 4 * (s % 2) + hh:11 + 4 * (s % 2) + hh])
                ins.then_inc(act_result_ready, 1)

        def conv(st):
            pass

        def attn(st):
            for s in range(16):
                n = (s // 8 + 1) * P
                act.wait_ge(act_input_ready, t_in.next())
                for part in range(2):
                    p = a_p[:, s // 2 % 2, s % 2, part, 0:n]
                    c = 8 + 8 * (s // 2 % 2) + 4 * (s % 2) + part
                    ins = act.activation(p, p, ACT.Exp, bias=stats[:, c:c + 1], accum_out=stats[:, c + 2:c + 3])
                ins.then_inc(act_result_ready, 1)
            act.wait_ge(act_input_ready, t_in.next())
            act.activation(stats[:, 0:16], stats[:, 0:16], ACT.Sqrt, scale=1.0 / (2 * ADH), bias=eps5)\
                .then_inc(act_result_ready, 1)

        def peer(st):
            def softmax_exp():
                act.wait_ge(act_input_ready, t_in.next())
                act.activation(p_if, p_if, ACT.Exp).then_inc(act_result_ready, 1)

            def gelus(lo, hi):
                g0 = st.which * TB * NSLOT + 2 * lo * GROUP
                with act.Fori(0, hi - lo) as it:
                    for q in range(2):
                        act.wait_ge(dot_done, it * (2 * GROUP) + (g0 + (q + 1) * GROUP + AHEAD))
                        act.activation(p_gel[:, q, :], p_dots[:, q, :], ACT.Gelu).then_inc(gelu_ready, 1)

            softmax_exp()
            gelus(0, CHOSEN)
            softmax_exp()
            gelus(CHOSEN, TB * NSLOT // (2 * GROUP))

        act.wait_ge(c_loaded, 32)
        act.activation(cact[:], cvec[:], ACT.Silu).then_inc(cact_ready, 1)
        act.wait_ge(act_input_ready, t_in.next())
        act.activation(rope[:], rope[:], ACT.Sin).then_inc(act_result_ready, 1)
        act.activation(lam2, lam2, ACT.Exp).then_inc(act_result_ready, 1)
        table = {"ffn": ffn, "gla": gla, "kv": kv, "mla": mla, "conv": conv, "attn": attn, "peer": peer}
        act.wait_ge(const_ready, 1)
        for st in stages:
            if st.n < 7:
                for b in range(TB):
                    act.wait_ge(x_ready, x_count(st.n) - TB + b + 1)
                    root_mean_square(st, x[:, b, :], b)
            table[st.kind](st)
            if st.n < 7 and st.kind != "kv":
                output_done(act, st)
                for b in range(TB):
                    root_mean_square(st, psF[:, b, :], b)
            if st.n >= 7:
                for b in range(TB):
                    act.wait_ge(var_ready, t_var.next())
                    act.activation(roots[:, b:b + 1], lnag[:, b, 1:2], ACT.Sqrt, bias=eps5).then_inc(root_ready, 1)

    @block.vector
    def _(dve):
        t_step, t_act, t_root = Turn(), Turn(), Turn()

        def link(ins):
            ins.then_inc(dve_step, 1)
            dve.wait_ge(dve_step, t_step.next())

        def full(u):
            dve.wait_ge(unit_full, u + 1)
            return psW[u % 3]

        def store(u, dst, src):
            full(u)
            dve.tensor_copy(dst, src).then_inc(unit_stored, 1)
            return u + 1

        def from_act(k=1):
            dve.wait_ge(act_result_ready, t_act.next(k))

        def store_row(st, j):
            dve.wait_ge(m_reduced, st.m + j + 1)
            kind, half = divmod(j, 2)
            dst = M[:, st.n % 2, kind, half * HALF:(half + 1) * HALF]
            if kind == 0:
                ins = dve.tensor_copy(dst, psM[:])
            elif st.n >= 7:
                ins = dve.tensor_scalar(dst, psM[:], 1.0, None, ALU.add)
            else:
                dve.wait_ge(g_loaded[st.n % 2], 32 * (st.n // 2 + 1))
                if kind == 1:
                    ins = dve.scalar_tensor_tensor(dst, psM[:], 1.0, dst, ALU.add, ALU.mult)
                else:
                    ins = dve.scalar_tensor_tensor(dst, psM[:], 0.5 if st.kind == "ffn" else 1.0, dst,
                                                   ALU.mult, ALU.mult)
            ins.then_inc(m_stored, 1)

        def hook(st, q, of):
            if st.n + 1 < len(stages):
                nx = stages[st.n + 1]
                for j in range(nx.mods * max(q - 1, 0) // of, nx.mods * q // of):
                    store_row(nx, j)

        def store_turned(u):
            for b in range(TB):
                for g in range(2):
                    ps = psW[u % 3][:].rearrange("p (j t) -> p j t", j=4)
                    u = store(u, hT[:, 4 * g:4 * g + 4, b * P:(b + 1) * P], ps)
            return u

        def prepare(st):
            dve.wait_ge(m_stored, st.m + st.mods)
            par = st.n % 2
            for b in range(TB):
                if st.n < 7:
                    dve.wait_ge(root_ready, t_root.next())
                    link(dve.reciprocal(roots[:, b:b + 1], roots[:, b:b + 1]))
                    link(dve.scalar_tensor_tensor(h[:, b, :], x[:, b, :], roots[:, b:b + 1], M[:, par, 1, :],
                                                  ALU.mult, ALU.mult))
                else:
                    dve.wait_ge(x_ready, x_count(st.n) - TB + b + 1)
                    link(dve.tensor_tensor(h[:, b, :], x[:, b, :], M[:, par, 1, :], ALU.mult))
                dve.tensor_tensor(h[:, b, :], h[:, b, :], M[:, par, 0, :], ALU.add).then_inc(h_ready, 1)

        def finish(st):
            par = st.n % 2
            if st.n < 7:
                for b in range(TB):
                    dve.wait_ge(root_ready, t_root.next())
                    link(dve.reciprocal(roots[:, b:b + 1], roots[:, b:b + 1]))
                    link(dve.scalar_tensor_tensor(h[:, b, :], psF[:, b, :], roots[:, b:b + 1], M[:, par, 2, :],
                                                  ALU.mult, ALU.mult))
                    dve.tensor_tensor(x[:, b, :], x[:, b, :], h[:, b, :], ALU.add).then_inc(x_ready, 1)
                return
            output_done(dve, st)
            dve.wait_ge(ln_loaded[par], 32 * ((st.n - 7) // 2 + 1))
            for b in range(TB):
                link(dve.tensor_tensor(h[:, b, :], psF[:, b, :], M[:, par, 2, :], ALU.mult))
                link(dve.scalar_tensor_tensor(x[:, b, :], x[:, b, :], ALPHA, h[:, b, :], ALU.mult, ALU.add))
                dve.bn_stats(lnst[:, b, 0, :], x[:, b, 0:HALF])
                link(dve.bn_stats(lnst[:, b, 1, :], x[:, b, HALF:]))
                dve.bn_aggr(lnag[:, b, :], lnst[:, b]).then_inc(var_ready, 1)
            for b in range(TB):
                dve.wait_ge(root_ready, t_root.next())
                link(dve.reciprocal(roots[:, b:b + 1], roots[:, b:b + 1]))
                link(dve.tensor_scalar(x[:, b, :], x[:, b, :], lnag[:, b, 0:1], roots[:, b:b + 1],
                                       ALU.subtract, ALU.mult))
                link(dve.tensor_tensor(x[:, b, :], x[:, b, :], ln[:, par, 0, :], ALU.mult))
                dve.tensor_tensor(x[:, b, :], x[:, b, :], ln[:, par, 1, :], ALU.add).then_inc(x_ready, 1)

        def ffn(st):
            u = store_turned(st.u)
            for j in range(FT):
                ps = full(u)
                dve.wait_ge(gate_ready, t_gate.next())
                dve.tensor_tensor(actT[:, j, :], sg[:, j % 2, :], ps[:, T:2 * T], ALU.mult).then_inc(unit_stored, 1)
                u += 1
                if j % 2:
                    hook(st, j // 2, 11)
            hook(st, 11, 11)

        def gla(st):
            u = store_turned(st.u)
            dve.memset(g_att, 0.0)
            u = store(u, g_low[0:GRANK, :], psW[u % 3][0:GRANK, 0:T])
            for j in range(4):
                dst = g_v if j < 2 else g_r
                for b in range(TB):
                    u = store(u, dst[:, b, (j % 2) * HALF:(j % 2 + 1) * HALF], psW[u % 3][:])
                if j == 0:
                    for b in range(TB):
                        u = store(u, g_la[:, b, :], psW[u % 3][:])
                if j == 1:
                    for b in range(TB):
                        from_act()
                        link(dve.scalar_tensor_tensor(g_la[:, b, :], g_la[:, b, :], 0.0, g_tmp[:, b, :],
                                                      ALU.min, ALU.subtract))
                        ins = dve.tensor_scalar(g_la[:, b, :], g_la[:, b, :], 1.0 / GTAU, None, ALU.mult)
                    ins.then_inc(state_ready, 1)
                hook(st, j, 6)
            for g in range(2):
                u = store(u, g_b[:, 2 * g:2 * g + 2, :], psW[u % 3][:].rearrange("p (a b) -> p a b", a=2))
            for j, dst in enumerate((g_q, g_k)):
                for g in range(2):
                    u = store(u, dst[:, 2 * g:2 * g + 2, :], psW[u % 3][:].rearrange("p (a b) -> p a b", a=2))
                hook(st, 4 + j, 6)
            from_act(4)
            dve.wait_ge(unit_stored, u)
            dec = stats[:, 16:32].rearrange("p (a b) -> p a b", a=GH)
            link(dve.tensor_copy(dec, g_eb.rearrange("p h (n c) -> p h n c", c=CH)[:, :, :, CH - 1]))
            dve.scalar_tensor_tensor(g_eb, g_q, GDK ** -0.5, g_eb, ALU.mult, ALU.mult)
            dve.tensor_tensor(g_en, g_k, g_en, ALU.mult)
            dve.tensor_tensor(g_eu, g_k, g_eu, ALU.mult).then_inc(state_ready, 1)
            for b in range(TB):
                u = store(u, g_ktok[:, b, :], psW[u % 3][:])
            for b in range(TB):
                ps = full(u)
                dve.copy_predicated(g_att[:, b], tri[:].bitcast(I32).unsqueeze(1).to_broadcast([P, GH, P]),
                                    ps[:].rearrange("p (a b) -> p a b", a=GH)).then_inc(unit_stored, 1)
                u += 1
            for n in range(NCH - 1):
                for g in range(2):
                    ps = full(u)[:].rearrange("p (a b) -> p a b", a=2)
                    if n == 0:
                        dve.tensor_copy(g_st[:, 0, 2 * g:2 * g + 2, :], ps).then_inc(unit_stored, 1)
                    else:
                        dve.wait_ge(unit_stored, u - 1)
                        for hh in range(2):
                            hd = 2 * g + hh
                            ins = dve.scalar_tensor_tensor(g_st[:, n, hd, :], g_st[:, n - 1, hd, :],
                                                           dec[:, hd, n:n + 1], ps[:, hh, :], ALU.mult, ALU.add)
                        ins.then_inc(unit_stored, 1)
                    u += 1
            for b in range(TB):
                for g in range(2):
                    u = store(u, h[:, b, g * HALF:(g + 1) * HALF], psW[u % 3][:])
            from_act()
            link(dve.reciprocal(stats[:, 0:8], stats[:, 0:8]))
            for b in range(TB):
                for hd in range(GH):
                    o = h[:, b, hd * GDV:(hd + 1) * GDV]
                    ins = dve.scalar_tensor_tensor(o, o, stats[:, 4 * b + hd:4 * b + hd + 1], gout[:],
                                                   ALU.mult, ALU.mult)
                link(ins)
                dve.tensor_tensor(h[:, b, :], h[:, b, :], g_r[:, b, :], ALU.mult).then_inc(h_ready, 1)
            u = store_turned(u)
            hook(st, 6, 6)

        def rotate(dst, src, b, heads, tmp):
            cs = [rope[:, i, b, :].unsqueeze(1).to_broadcast([P, heads, ROPE // 2]) for i in range(2)]
            x1, x2 = src[:, :, 0:ROPE // 2], src[:, :, ROPE // 2:ROPE]
            y1, y2 = dst[:, :, 0:ROPE // 2], dst[:, :, ROPE // 2:ROPE]
            dve.tensor_tensor(y1, x1, cs[0], ALU.mult)
            dve.tensor_tensor(y2, x1, cs[1], ALU.mult)
            dve.tensor_tensor(tmp[:, 0], x2, cs[1], ALU.mult)
            link(dve.tensor_tensor(tmp[:, 1], x2, cs[0], ALU.mult))
            dve.tensor_tensor(y1, y1, tmp[:, 0], ALU.subtract)
            return dve.tensor_tensor(y2, y2, tmp[:, 1], ALU.add)

        def kv(st):
            u = store_turned(st.u)
            dve.memset(krT[ROPE:, 0, :], 0.0)
            dve.memset(krT[0:ROPE, 1, :], 0.0)
            for b in range(TB):
                u = store(u, kv_raw[:, b, :], psW[u % 3][:, 0:KVL + ROPE])
            for b in range(TB):
                from_act()
                link(dve.reciprocal(stats[:, b:b + 1], stats[:, b:b + 1]))
                dve.scalar_tensor_tensor(kv_c[:, b, :], kv_raw[:, b, 0:KVL], stats[:, b:b + 1], g_kv,
                                         ALU.mult, ALU.mult)
                tmp = view(2048, 2, 1, ROPE // 2)
                link(rotate(kv_r[:, b:b + 1, 0:ROPE], kv_raw[:, b:b + 1, KVL:], b, 1, tmp))
                dve.tensor_copy(kv_r[:, b, ROPE:], kv_r[:, b, 0:ROPE]).then_inc(yT_ready, 1)
                hook(st, b, TB + 1)
            for b in range(TB):
                ps = full(u)
                dve.tensor_copy(kv_cT[:, :, b * P:(b + 1) * P], ps[:, 0:2 * P].rearrange("p (a b) -> p a b", a=2))
                dve.tensor_copy(krT[0:ROPE, 0, b * P:(b + 1) * P], ps[0:ROPE, 2 * P:3 * P])
                dve.tensor_copy(krT[ROPE:, 1, b * P:(b + 1) * P], ps[ROPE:, 2 * P:3 * P]).then_inc(unit_stored, 1)
                u += 1
            hook(st, TB, TB + 1)
            for j in range(2):
                for g in range(2):
                    u = store(u, knT[:, 4 * j + 2 * g:4 * j + 2 * g + 2, :],
                              psW[u % 3][:].rearrange("p (a b) -> p a b", a=2))
                for b in range(TB):
                    u = store(u, vmla[:, b, j * HALF:(j + 1) * HALF], psW[u % 3][:])
            hook(st, TB + 1, TB + 1)

        def mla(st):
            u = store_turned(st.u)
            dve.tensor_scalar(m_mask, dist[:], 1e30, NEG, ALU.is_ge, ALU.mult)
            for b in range(TB):
                u = store(u, m_c[:, b, :], psW[u % 3][:, 0:QL])
            hook(st, 0, 3)
            for b in range(TB):
                from_act()
                link(dve.reciprocal(stats[:, b:b + 1], stats[:, b:b + 1]))
                dve.scalar_tensor_tensor(m_c[:, b, :], m_c[:, b, :], stats[:, b:b + 1], g_ql,
                                         ALU.mult, ALU.mult).then_inc(yT_ready, 1)
            for b in range(TB):
                u = store(u, m_cT[:, :, b * P:(b + 1) * P], psW[u % 3][:, 0:QL].rearrange("p (a b) -> p a b", a=3))
            for g in range(4):
                u = store(u, m_qnT[:, 2 * g:2 * g + 2, :], psW[u % 3][:].rearrange("p (a b) -> p a b", a=2))
            hook(st, 1, 3)
            for b in range(TB):
                u = store(u, m_t[:, 2 * b:2 * b + 2, :], psW[u % 3][:].rearrange("p (a b) -> p a b", a=2))
            dve.wait_ge(unit_stored, u)
            for b in range(TB):
                raw = m_t[:, 2 * b:2 * b + 2, :].rearrange("p a (h c) -> p (a h) c", c=ROPE)
                dst = m_qr[:, b, :].rearrange("p (h c) -> p h c", c=ROPE)
                tmp = h[:, b, 0:512].rearrange("p (a h c) -> p a h c", a=2, h=MH)
                rotate(dst, raw, b, MH, tmp).then_inc(yT_ready, 1)
            hook(st, 2, 3)
            for b in range(TB):
                u = store(u, m_qrT[:, :, b * P:(b + 1) * P], psW[u % 3][:].rearrange("p (a b) -> p a b", a=4))

            def masked(u, s):
                n = (s // 4 + 1) * P
                ps = full(u)[:].rearrange("p (a b) -> p a b", a=2)
                p = m_p[:, s % 2, :, 0:n]
                c = 8 + 4 * (s % 2)
                dve.scalar_tensor_tensor(p, ps[:, :, 0:n], (NOPE + ROPE) ** -0.5,
                                         m_mask[:, 2 * P - n:].unsqueeze(1).to_broadcast([P, 2, n]),
                                         ALU.mult, ALU.add).then_inc(unit_stored, 1)
                u += 1
                dve.wait_ge(unit_stored, u)
                dve.reduce_max(stats[:, c:c + 2], p, AX, negate=True).then_inc(act_input_ready, 1)
                return u

            u = masked(u, 0)
            for s in range(8):
                b, g = divmod(s, 4)
                if s + 1 < 8:
                    u = masked(u, s + 1)
                p, c = m_p[:, s % 2, :, 0:(b + 1) * P], 8 + 4 * (s % 2)
                from_act()
                link(dve.reciprocal(stats[:, c + 2:c + 4], stats[:, c + 2:c + 4]))
                for hh in range(2):
                    ins = dve.tensor_scalar(p[:, hh, :], p[:, hh, :], stats[:, c + 2 + hh:c + 3 + hh], None, ALU.mult)
                ins.then_inc(att_ready, 1)
                src = psW[u % 3][:].rearrange("p (h k t) -> p h k t", h=2, k=2)[:, :, 0:b + 1, :]
                dst = m_pT[:, s % 2].rearrange("p (h k) t -> p h k t", h=2)[:, :, 0:b + 1, :]
                u = store(u, dst, src)
                u = store(u, hT[:, 2 * g:2 * g + 2, b * P:(b + 1) * P],
                          psW[u % 3][:, 0:2 * P].rearrange("p (a b) -> p a b", a=2))
            hook(st, 3, 3)

        def conv(st):
            u = store_turned(st.u)
            u = store(u, c_w, psW[u % 3][:, 0:24])
            dve.memset(c_z[:, :, 0:2], 0.0)
            for j in range(6):
                for g in range(2):
                    ps = psW[u % 3][:].rearrange("p (a b) -> p a b", a=2)
                    k = 4 * (j % 2) + 2 * g
                    if j < 4:
                        u = store(u, (c_gb if j < 2 else c_gc)[:, k:k + 2, :], ps)
                    else:
                        full(u)
                        dve.tensor_tensor(c_z[:, k:k + 2, 2:], c_gc[:, k:k + 2, :], ps, ALU.mult)\
                            .then_inc(unit_stored, 1)
                        u += 1
                hook(st, j, 6)
            dve.wait_ge(unit_stored, u)
            for w in range(3):
                for k in range(KD):
                    z, c = c_z[:, k, w:w + T], c_w[:, w * KD + k:w * KD + k + 1]
                    if w == 0:
                        ins = dve.tensor_scalar(c_gc[:, k, :], z, c, None, ALU.mult)
                    else:
                        ins = dve.scalar_tensor_tensor(c_gc[:, k, :], z, c, c_gc[:, k, :], ALU.mult, ALU.add)
                link(ins)
            dve.tensor_tensor(c_gc, c_gc, c_gb, ALU.mult).then_inc(yT_ready, 1)
            hook(st, 6, 6)

        def attn(st):
            u = store_turned(st.u)
            dve.memset(a_k[ADH:, :, 0, :], 0.0)
            dve.memset(a_k[0:ADH, :, 1, :], 0.0)
            for j in range(6):
                for g in range(2):
                    k = 4 * (j % 2) + 2 * g
                    ps = psW[u % 3][:].rearrange("p (a b) -> p a b", a=2)
                    if j < 2:
                        u = store(u, a_q[:, k:k + 2, :], ps)
                    elif j < 4:
                        full(u)
                        dve.tensor_copy(a_k[0:ADH, k:k + 2, 0, :], ps[0:ADH])
                        u = store(u, a_k[ADH:, k:k + 2, 1, :], ps[ADH:])
                    else:
                        u = store(u, a_v[:, g, (j - 4) * HALF:(j - 3) * HALF], psW[u % 3][:])
                hook(st, j, 6)

            def biased(u, s):
                b, g = divmod(s, 4)
                n = (b + 1) * P
                for hh in range(2):
                    hd = 2 * g + hh
                    link(dve.tensor_scalar(a_d[:, hh, 0:n], dist[:, 2 * P - n:], -(2.0 ** -(hd + 1)), None, ALU.mult))
                    ps = full(u)[:].rearrange("p (a b) -> p a b", a=2)
                    p = a_p[:, s % 2, hh, :, 0:n]
                    c = 8 + 8 * (s % 2) + 4 * hh
                    dve.scalar_tensor_tensor(p, ps[:, :, 0:n], ADH ** -0.5,
                                             a_d[:, hh, 0:n].unsqueeze(1).to_broadcast([P, 2, n]),
                                             ALU.mult, ALU.add).then_inc(unit_stored, 1)
                    u += 1
                    dve.wait_ge(unit_stored, u)
                    dve.reduce_max(stats[:, c:c + 2], p, AX, negate=True).then_inc(act_input_ready, 1)
                return u

            u = biased(u, 0)
            for s in range(8):
                b, g = divmod(s, 4)
                if s + 1 < 8:
                    u = biased(u, s + 1)
                for hh in range(2):
                    p = a_p[:, s % 2, hh, :, 0:(b + 1) * P]
                    c = 8 + 8 * (s % 2) + 4 * hh
                    from_act()
                    link(dve.reciprocal(stats[:, c + 2:c + 4], stats[:, c + 2:c + 4]))
                    link(dve.tensor_scalar(p[:, 1, :], p[:, 1, :], stats[:, c + 3:c + 4], neg_lam, ALU.mult, ALU.mult))
                    ins = dve.scalar_tensor_tensor(p[:, 0, :], p[:, 0, :], stats[:, c + 2:c + 3], p[:, 1, :],
                                                   ALU.mult, ALU.add)
                ins.then_inc(att_ready, 1)
                src = psW[u % 3][:].rearrange("p (h k t) -> p h k t", h=2, k=2)[:, :, 0:b + 1, :]
                dst = a_pT[:, s % 2].rearrange("p (h k) t -> p h k t", h=2)[:, :, 0:b + 1, :]
                u = store(u, dst, src)
                u = store(u, h[:, b, 2 * g * P:(2 * g + 2) * P], psW[u % 3][:, 0:2 * P])
            dve.wait_ge(unit_stored, u)
            sq = arena[:, 0:TB * D]
            hv = h[:].rearrange("p b n -> p (b n)")
            link(dve.tensor_tensor(sq, hv, hv, ALU.mult))
            dve.tensor_reduce(stats[:, 0:16], sq.rearrange("p (a b) -> p a b", b=P), AX, ALU.add)\
                .then_inc(act_input_ready, 1)
            from_act()
            link(dve.reciprocal(stats[:, 0:16], stats[:, 0:16]))
            for b in range(TB):
                o = h[:, b, :].rearrange("p (a b) -> p a b", b=P)
                link(dve.tensor_tensor(o, o, stats[:, 8 * b:8 * b + 8].unsqueeze(2).to_broadcast([P, 8, P]), ALU.mult))
                dve.scalar_tensor_tensor(o, o, 1.0 - LAMBDA_INIT, g_sub.unsqueeze(1).to_broadcast([P, 8, P]),
                                         ALU.mult, ALU.mult).then_inc(h_ready, 1)
            u = store_turned(u)
            hook(st, 6, 6)

        def top16(vals, best, where, groups):
            for half in range(2):
                sl = slice(8 * half, 8 * half + 8)
                for g in range(groups):
                    ins = dve.max(best[:, g, sl], vals[:, g, :])
                link(ins)
                for g in range(groups):
                    ins = dve.max_index(where[:, g, sl], best[:, g, sl], vals[:, g, :])
                if half == 0:
                    for g in range(groups):
                        ins = dve.match_replace(vals[:, g, :], best[:, g, sl], vals[:, g, :], NEG)
                link(ins)
                yield

        def choose(st, b):
            yield from top16(p_sc, p_sv, p_si, 2 * PH)
            dve.tensor_copy(p_sf, p_si)
            sv = p_sv.rearrange("p (h s) k -> p h s k", s=2)
            sf = p_sf.rearrange("p (h s) k -> p h s k", s=2)
            cand = arena[:, 6144:8192].rearrange("p (h i j) -> p h i j", h=PH, i=PK)
            link(dve.tensor_tensor(cand, sv[:, :, 0, :].unsqueeze(3).to_broadcast([P, PH, PK, PK]),
                                   sv[:, :, 1, :].unsqueeze(2).to_broadcast([P, PH, PK, PK]), ALU.add))
            yield from top16(cand.rearrange("p h i j -> p h (i j)"), p_ts, p_pos.rearrange("p (h k) -> p h k", h=PH), PH)
            for s in range(2):
                if s == 0:
                    link(dve.tensor_scalar(p_ij, p_pos, 4, None, ALU.logical_shift_right))
                else:
                    link(dve.tensor_scalar(p_ij, p_pos, 15, None, ALU.bitwise_and))
                link(dve.tensor_copy(p_if, p_ij))
                link(dve.tensor_tensor(p_oh, p_if.unsqueeze(2).to_broadcast([P, NSLOT, PK]),
                                       p_iota.unsqueeze(1).to_broadcast([P, NSLOT, PK]), ALU.is_equal))
                oh = p_oh.rearrange("p (h k) i -> p h k i", h=PH)
                link(dve.tensor_tensor(oh, oh, sf[:, :, s, :].unsqueeze(2).to_broadcast([P, PH, PK, PK]), ALU.mult))
                link(dve.tensor_reduce(p_e[:, s, :], p_oh, AX, ALU.add))
            link(dve.scalar_tensor_tensor(p_e[:, 0, :], p_e[:, 0, :], float(NK), p_e[:, 1, :], ALU.mult, ALU.add))
            dve.tensor_scalar(p_idx[:, b * NSLOT:(b + 1) * NSLOT], p_e[:, 0, :], float(st.which * NK * NK), None, ALU.add)
            lg = p_if.rearrange("p (h k) -> p h k", h=PH)
            dve.tensor_tensor(lg, p_ts, p_ts[:, :, 0:1].to_broadcast([P, PH, PK]), ALU.subtract)\
                .then_inc(act_input_ready, 1)
            from_act()
            link(dve.tensor_reduce(stats[:, 0:PH], lg, AX, ALU.add))
            link(dve.reciprocal(stats[:, 0:PH], stats[:, 0:PH]))
            link(dve.tensor_tensor(p_g[:, b, :].rearrange("p (h k) -> p h k", h=PH), lg,
                                   stats[:, 0:PH].unsqueeze(2).to_broadcast([P, PH, PK]), ALU.mult))

        def peer(st):
            def rows(b, lo, hi):
                first = (st.which * TB + b) * (NSLOT // GROUP) + 2 * lo
                with dve.Fori(0, hi - lo) as it:
                    for q in range(2):
                        group = it * 2 + (first + q)
                        for s in range(GROUP):
                            dve.wait_ge(u_loaded[s], group * 16 + 16)
                            dve.wait_ge(dot_done, group * GROUP + (max(s - 1, 0) + AHEAD))
                            dve.scalar_tensor_tensor(p_junk[:, s % 2, :], row_u(s), 1.0, h[:, b, :], ALU.mult, ALU.mult,
                                                     accum_out=p_dots[:, q, s:s + 1]).then_inc(dot_done, 1)
                        dve.wait_ge(v_used, group * GROUP + AHEAD)
                        nxt = it * (2 * GROUP) + (b * NSLOT + (2 * lo + q + 1) * GROUP)
                        dve.tensor_copy(p_icur[:, 1 - q, :], p_idx[:, bass.ds(nxt, GROUP)]).then_inc(idx_ready, 1)
                        dve.wait_ge(gelu_ready, group + 1)
                        cur = it * (2 * GROUP) + (2 * lo + q) * GROUP
                        dve.tensor_tensor(p_w[:, q, :], p_gel[:, q, :], p_g[:, b, bass.ds(cur, GROUP)],
                                          ALU.mult).then_inc(w_ready, 1)
                        dve.wait_ge(w_ready, group + 1)
                        for s in range(GROUP):
                            dve.tensor_scalar(p_diag[:, s, :], ident[:], p_w[:, q, s:s + 1], None, ALU.mult)\
                                .then_inc(diag_ready, 1)

            def query(u, j, b):
                return store(u, p_qT[:, 4 * j:4 * j + 4, b * P:(b + 1) * P],
                             psW[u % 3][:].rearrange("p (a b) -> p a b", a=4))

            def score(u):
                for g in range(4):
                    u = store(u, p_sc[:, 4 * g:4 * g + 4, :], psW[u % 3][:].rearrange("p (a b) -> p a b", a=4))
                dve.wait_ge(unit_stored, u)
                return u

            u = store_turned(st.u)
            for j in range(4):
                u = query(u, j, 0)
                hook(st, j, 4)
            u = store(u, p_skT, psW[u % 3][:, 0:2 * P].rearrange("p (a b) -> p a b", a=2))
            u = score(u)
            for j, _ in enumerate(choose(st, 0)):
                u = query(u, j, 1)
                if j == 0:
                    hook(st, 4, 4)
            dve.tensor_copy(p_icur[:, 0, :], p_idx[:, 0:GROUP]).then_inc(idx_ready, 1)
            u = score(u)
            dve.memset(p_idx[:, TB * NSLOT:], 0)
            pairs, done = NSLOT // (2 * GROUP), 0
            for j, _ in enumerate(choose(st, 1)):
                if j % 2 == 0:
                    rows(0, done, done + 2)
                    done += 2
            rows(0, done, pairs)
            rows(1, 0, pairs)

        t_gate = Turn()
        dve.sem_inc(dot_done, AHEAD)
        dve.wait_ge(cact_ready, 1)
        dve.tensor_copy(cb, cact[:, 0, :].unsqueeze(2).to_broadcast([P, KD, P])).then_inc(cb_ready, 1)
        dve.wait_ge(const_ready, 1)
        dve.wait_ge(misc_loaded, 16 * MISC)
        posf, ang, kk = small[:, 10:12], view(0, TB, 32), view(64, 2, 64)
        rv = rope[:].rearrange("p s b c -> p s (b c)")
        angf = arena[:, 0:64]
        link(dve.tensor_copy(posf, small[:, 8:10].bitcast(I32)))
        for b in range(TB):
            ins = dve.tensor_scalar(ang[:, b, :], invf[:], posf[:, b:b + 1], None, ALU.mult)
        link(ins)
        magic = 1.5 * 2.0 ** 23
        for s in range(2):
            ins = dve.tensor_scalar(kk[:, s, :], angf, 1.0 / (2 * np.pi), 0.25 * (1 - s), ALU.mult, ALU.add)
        link(ins)
        link(dve.tensor_scalar(kk, kk, magic, None, ALU.add))
        link(dve.tensor_scalar(kk, kk, -magic, None, ALU.add))
        link(dve.scalar_tensor_tensor(rv, kk, -6.28125, angf.unsqueeze(1).to_broadcast([P, 2, 64]), ALU.mult, ALU.add))
        c2 = 0.00193500518798828125
        link(dve.scalar_tensor_tensor(rv, kk, -c2, rv, ALU.mult, ALU.add))
        link(dve.scalar_tensor_tensor(rv, kk, -(2 * np.pi - 6.28125 - c2), rv, ALU.mult, ALU.add))
        link(dve.tensor_scalar(rv[:, 0, :], rv[:, 0, :], np.pi / 2, None, ALU.add))
        link(dve.tensor_scalar(rv, rv, 3.1415925, -3.1415925, ALU.min, ALU.max))
        lv = lamt[:].rearrange("p (a b c) -> p a b c", a=2, b=2)
        lp = view(256, 2, ADH)
        link(dve.tensor_tensor(lp, lv[:, :, 0, :], lv[:, :, 1, :], ALU.mult))
        dve.tensor_reduce(lam2, lp, AX, ALU.add).then_inc(act_input_ready, 1)
        from_act(2)
        link(dve.tensor_tensor(neg_lam, lam2[:, 1:2], lam2[:, 0:1], ALU.subtract))
        link(dve.tensor_scalar(neg_lam, neg_lam, -LAMBDA_INIT, None, ALU.add))
        dve.wait_ge(x_loaded, 16)
        dve.sem_inc(x_ready, TB)
        for j in range(stages[0].mods):
            store_row(stages[0], j)
        table = {"ffn": ffn, "gla": gla, "kv": kv, "mla": mla, "conv": conv, "attn": attn, "peer": peer}
        for st in stages:
            prepare(st)
            table[st.kind](st)
            if st.kind != "kv":
                finish(st)


_INS = ["x", "c", "positions", "cond_w", "cond_b", "norm_g", "ffn_w_gu", "ffn_w_down", "gla_w_in",
        "gla_w_gate_up", "gla_b_gate", "gla_g_out", "gla_w_out", "kv_g_in", "kv_cond_w", "kv_cond_b",
        "mla_w_kv_a", "mla_g_kv", "mla_w_kv_b", "mla_w_dq", "mla_g_q", "mla_w_uq", "mla_w_out",
        "c_2", "ada_w_2", "ada_b_2", "ln_g_2", "ln_b_2", "conv_w_in_2", "conv_w_2", "conv_w_out_2",
        "attn_w_qkv_2", "attn_lambda_2", "attn_subln_g_2", "attn_w_o_2", "peer_w_q_2",
        "peer_sub_keys_2", "peer_u_2", "peer_v_2"]


def kernel(**inputs):
    import concourse.bacc as _bacc
    from concourse.bass_utils import run_bass_kernel_spmd as _run

    nc = _bacc.Bacc("TRN2", target_bir_lowering=False, num_devices=1)
    arrays, args = {}, {}
    given = {name: np.ascontiguousarray(inputs[name]) for name in _INS}
    given["inv_freq"] = (np.float32(THETA) ** (-np.arange(0, ROPE, 2, dtype=np.float32) / np.float32(ROPE)))\
        .astype(np.float32)
    for name, v in given.items():
        arrays[f"in_{name}_dram"] = v
        args[name] = nc.dram_tensor(f"in_{name}_dram", v.shape, mybir.dt.from_np(v.dtype), kind="ExternalInput").ap()
    out = nc.dram_tensor("out_0_dram", (1, T, D), F32, kind="ExternalOutput").ap()
    build(nc, args, out)
    r = _run(nc, [arrays], core_ids=[0])
    return r.results[0]["out_0_dram"]
```
